# Optimizing a Trainium2 kernel written in Bass

```python
import functools
import jax, jax.numpy as jnp
from jax import lax
import numpy as np

D_MODEL = 1024
BATCH = 1
SEQ = 1024
DEPTH = 1
DEC_BATCH = 1
DEC_SEQ = 32
PAST_LEN = 512

CHUNK = 64
LEFT_CHUNKS = 8
D_MIX = D_MODEL
D_ATTN = D_MIX // 2
D_POOL = D_MIX - D_ATTN
HEAD_DIM = 64
N_HEADS = D_ATTN // HEAD_DIM
ATTN_SCALE = HEAD_DIM ** -0.5
REL_CLIP = 128
N_REL = 2 * REL_CLIP + 1
POOL_WINDOWS = (2, 4, 8, 16)
N_POOL_GROUPS = len(POOL_WINDOWS)
POOL_GROUP_DIM = D_POOL // N_POOL_GROUPS
POOL_HIST = max(POOL_WINDOWS) - 1
D_IN = 3 * D_ATTN + D_POOL
D_FF = 4 * D_MODEL
D_PLE = 256
EPS = 1e-6
NEG_INF = -1e30

kernel_name = "hybrid_chunk_band_attn_pool_streaming_step"

def rmsnorm(x, g):
    xf = x.astype(jnp.float32)
    y = xf * lax.rsqrt(jnp.mean(xf * xf, axis=-1, keepdims=True) + EPS)
    return (y * g.astype(jnp.float32)).astype(x.dtype)

def band_attention(q, kb, vb, qpos, kpos, kvalid, rel_bias):
    s = jnp.einsum("bnqhd,bnkhd->bnhqk", q, kb).astype(jnp.float32) * ATTN_SCALE
    rel = jnp.clip(qpos[:, :, None] - kpos[:, None, :], -REL_CLIP, REL_CLIP) + REL_CLIP
    bias = jnp.moveaxis(jnp.take(rel_bias.astype(jnp.float32), rel, axis=1), 0, 1)
    s = jnp.where(kvalid[None, :, None, None, :], s + bias[None], NEG_INF)
    pr = jax.nn.softmax(s, axis=-1).astype(vb.dtype)
    return jnp.einsum("bnhqk,bnkhd->bnqhd", pr, vb)

def multiscale_pool(u_ext, n_hist, w_pool, pool_scale):
    B, L, C = u_ext.shape
    T = L - n_hist
    cs = jnp.concatenate([jnp.zeros((B, 1, C), jnp.float32),
                          jnp.cumsum(u_ext.astype(jnp.float32), axis=1)], axis=1)
    idx = n_hist + jnp.arange(T)
    outs = []
    for g, w in enumerate(POOL_WINDOWS):
        lo, hi = g * POOL_GROUP_DIM, (g + 1) * POOL_GROUP_DIM
        start = jnp.maximum(idx + 1 - w, 0)
        cnt = (idx + 1 - start).astype(jnp.float32)
        csg = cs[:, :, lo:hi]
        mean = (csg[:, idx + 1] - csg[:, start]) / cnt[None, :, None]
        diff = (mean - u_ext[:, n_hist:, lo:hi].astype(jnp.float32)).astype(u_ext.dtype)
        outs.append(jnp.einsum("btc,cd->btd", diff, w_pool[g]))
    return jnp.concatenate(outs, axis=-1) * pool_scale

def prompt_mixer(q, k, v, u, rel_bias, w_pool, pool_scale):
    B, T, H, Dh = q.shape
    nc = T // CHUNK
    left = LEFT_CHUNKS * CHUNK
    band = left + CHUNK
    pad = ((0, 0), (left, 0), (0, 0), (0, 0))
    kp = jnp.pad(k, pad)
    vp = jnp.pad(v, pad)
    idx = (jnp.arange(nc) * CHUNK)[:, None] + jnp.arange(band)[None, :]
    kpos = idx - left
    qpos = jnp.arange(T).reshape(nc, CHUNK)
    attn = band_attention(q.reshape(B, nc, CHUNK, H, Dh), kp[:, idx], vp[:, idx],
                          qpos, kpos, kpos >= 0, rel_bias).reshape(B, T, H * Dh)
    pool = multiscale_pool(u, 0, w_pool, pool_scale)
    keep = min(left, T)
    return attn, pool, (k[:, T - keep:], v[:, T - keep:], u[:, T - POOL_HIST:])

def sample_mixer(q, k, v, u, cache_k, cache_v, state_pool, rel_bias, w_pool, pool_scale):
    B, T, H, Dh = q.shape
    win = cache_k.shape[1]
    kb = jnp.concatenate([cache_k.astype(k.dtype), k], axis=1)[:, None]
    vb = jnp.concatenate([cache_v.astype(v.dtype), v], axis=1)[:, None]
    qpos = (PAST_LEN + jnp.arange(T))[None]
    kpos = (PAST_LEN - win + jnp.arange(win + T))[None]
    attn = band_attention(q[:, None], kb, vb, qpos, kpos, jnp.ones(kpos.shape, bool),
                          rel_bias).reshape(B, T, H * Dh)
    u_ext = jnp.concatenate([state_pool.astype(u.dtype), u], axis=1)
    pool = multiscale_pool(u_ext, POOL_HIST, w_pool, pool_scale)
    return attn, pool, (k, v, u_ext[:, -POOL_HIST:])

def trunk_layer(x, p, mixer, g_mix_pre, g_mix_post, g_ff_pre, g_ff_post, g_ple_post,
                w_in, w_out, w_ff1, w_ff2, w_ple, w_ple_gate):
    B, T, _ = x.shape
    h = rmsnorm(x, g_mix_pre)
    qkvu = jnp.einsum("btd,de->bte", h, w_in)
    q = qkvu[..., :D_ATTN].reshape(B, T, N_HEADS, HEAD_DIM)
    k = qkvu[..., D_ATTN:2 * D_ATTN].reshape(B, T, N_HEADS, HEAD_DIM)
    v = qkvu[..., 2 * D_ATTN:3 * D_ATTN].reshape(B, T, N_HEADS, HEAD_DIM)
    u = qkvu[..., 3 * D_ATTN:]
    attn, pool, state = mixer(q, k, v, u)
    mix = jnp.einsum("bte,ed->btd", jnp.concatenate([attn, pool], axis=-1), w_out)
    x = x + rmsnorm(mix, g_mix_post)
    hf = jnp.einsum("btd,df->btf", rmsnorm(x, g_ff_pre), w_ff1)
    ff = jnp.einsum("btf,fd->btd", jnp.square(jax.nn.relu(hf)), w_ff2)
    x = x + rmsnorm(ff, g_ff_post)
    gate = jax.nn.sigmoid(jnp.einsum("btd,de->bte", x, w_ple_gate))
    ple = gate * jnp.einsum("btp,pd->btd", p, w_ple)
    x = x + rmsnorm(ple, g_ple_post)
    return x, state

def setup_inputs(seed: int = 0) -> dict:
    key = jax.random.key(seed)
    ks = jax.random.split(key, 32)
    f32 = jnp.float32
    kv_win = min(LEFT_CHUNKS * CHUNK, PAST_LEN)

    def nrm(k, shape, scale):
        return scale * jax.random.normal(k, shape, f32)

    def gain(k, n):
        return 1.0 + 0.05 * jax.random.normal(k, (DEPTH, n), f32)

    return {
        "x_prompt": nrm(ks[0], (BATCH, SEQ, D_MODEL), 1.0),
        "x_sample": nrm(ks[1], (DEC_BATCH, DEC_SEQ, D_MODEL), 1.0),
        "cache_k": nrm(ks[2], (DEPTH, DEC_BATCH, kv_win, N_HEADS, HEAD_DIM), 1.0),
        "cache_v": nrm(ks[3], (DEPTH, DEC_BATCH, kv_win, N_HEADS, HEAD_DIM), 1.0),
        "state_pool": nrm(ks[4], (DEPTH, DEC_BATCH, POOL_HIST, D_POOL), 1.0),
        "p_prompt": nrm(ks[5], (DEPTH, BATCH, SEQ, D_PLE), 1.0),
        "p_sample": nrm(ks[6], (DEPTH, DEC_BATCH, DEC_SEQ, D_PLE), 1.0),
        "g_mix_pre": gain(ks[7], D_MODEL),
        "g_mix_post": gain(ks[8], D_MODEL),
        "g_ff_pre": gain(ks[9], D_MODEL),
        "g_ff_post": gain(ks[10], D_MODEL),
        "g_ple_post": gain(ks[11], D_MODEL),
        "w_in": nrm(ks[12], (DEPTH, D_MODEL, D_IN), D_MODEL ** -0.5),
        "rel_bias": nrm(ks[13], (DEPTH, N_HEADS, N_REL), 0.1),
        "w_pool": nrm(ks[14], (DEPTH, N_POOL_GROUPS, POOL_GROUP_DIM, POOL_GROUP_DIM), POOL_GROUP_DIM ** -0.5),
        "pool_scale": 1.0 + 0.1 * jax.random.normal(ks[15], (DEPTH, D_POOL), f32),
        "w_out": nrm(ks[16], (DEPTH, D_MIX, D_MODEL), D_MIX ** -0.5),
        "w_ff1": nrm(ks[17], (DEPTH, D_MODEL, D_FF), D_MODEL ** -0.5),
        "w_ff2": nrm(ks[18], (DEPTH, D_FF, D_MODEL), D_FF ** -0.5),
        "w_ple": nrm(ks[19], (DEPTH, D_PLE, D_MODEL), D_PLE ** -0.5),
        "w_ple_gate": nrm(ks[20], (DEPTH, D_MODEL, D_MODEL), D_MODEL ** -0.5),
    }

def reference(x_prompt, x_sample, cache_k, cache_v, state_pool, p_prompt, p_sample,
              g_mix_pre, g_mix_post, g_ff_pre, g_ff_post, g_ple_post,
              w_in, rel_bias, w_pool, pool_scale, w_out, w_ff1, w_ff2, w_ple, w_ple_gate):
    xp, xs = x_prompt, x_sample
    kp_l, vp_l, up_l, ks_l, vs_l, us_l = [], [], [], [], [], []
    for i in range(DEPTH):
        shared = (g_mix_pre[i], g_mix_post[i], g_ff_pre[i], g_ff_post[i], g_ple_post[i],
                  w_in[i], w_out[i], w_ff1[i], w_ff2[i], w_ple[i], w_ple_gate[i])
        mix_p = functools.partial(prompt_mixer, rel_bias=rel_bias[i], w_pool=w_pool[i],
                                  pool_scale=pool_scale[i])
        mix_s = functools.partial(sample_mixer, cache_k=cache_k[i], cache_v=cache_v[i],
                                  state_pool=state_pool[i], rel_bias=rel_bias[i],
                                  w_pool=w_pool[i], pool_scale=pool_scale[i])
        xp, (kp, vp, up) = trunk_layer(xp, p_prompt[i], mix_p, *shared)
        xs, (kn, vn, un) = trunk_layer(xs, p_sample[i], mix_s, *shared)
        kp_l.append(kp); vp_l.append(vp); up_l.append(up)
        ks_l.append(kn); vs_l.append(vn); us_l.append(un)
    k_prompt_new = jnp.stack(kp_l)
    v_prompt_new = jnp.stack(vp_l)
    pool_prompt_new = jnp.stack(up_l)
    k_sample_new = jnp.stack(ks_l)
    v_sample_new = jnp.stack(vs_l)
    pool_sample_new = jnp.stack(us_l)
    return (xp, xs, k_prompt_new, v_prompt_new, pool_prompt_new, k_sample_new, v_sample_new, pool_sample_new)


_drawn_inputs = setup_inputs


def setup_inputs(seed=0):
    import zlib

    import numpy as np

    out = dict(_drawn_inputs(seed))
    spreads = {}
    factors = {'rel_bias': 7.813}
    for name, (base, spread) in spreads.items():
        noise = np.random.default_rng([zlib.crc32(name.encode()), seed]).standard_normal(out[name].shape)
        drawn = base * np.exp(spread * noise) if base else spread * noise
        out[name] = __import__('jax').numpy.asarray(drawn.astype(out[name].dtype))
    for name, factor in factors.items():
        out[name] = (out[name] * factor).astype(out[name].dtype)
    return out
```

```python
from contextlib import ExitStack

import concourse.bass as bass
from concourse import mybir

F32 = mybir.dt.float32
F32R = mybir.dt.float32r
ALU = mybir.AluOpType
ACT = mybir.ActivationFunctionType

P = 128
D_MODEL = 1024
KT = D_MODEL // P
SEQ, DEC = 1024, 32
TOK = SEQ + DEC
NB, BW = 3, TOK // 3
CHUNK, LEFT = 64, 512
N_HEADS, HEAD = 8, 64
PAIRS = N_HEADS // 2
WIN = LEFT + 2 * CHUNK
CACHE = 512
SKEYS = CACHE + DEC
EXT = WIN + P - 1
POOL_WINDOWS = (2, 4, 8, 16)
GROUPS = len(POOL_WINDOWS)
HIST = max(POOL_WINDOWS) - 1
UCOLS = HIST + SEQ + HIST + DEC
FF_CHUNKS = 4
EPS = 1e-6
NEG = -1e30
QSCALE = HEAD ** -0.5

ABLK = ((0, 384), (384, 384), (768, 288))
SAMPLE_UNIT = SEQ // P
UNITS = SAMPLE_UNIT + 1
BLOCKS = 9
Q, V, K = 0, 1, 2

W_U = GROUPS
D_OUT = 4
D_FF = D_OUT + KT
D_GATE = D_FF + 2 * KT * FF_CHUNKS
D_END = D_GATE + KT
W_OF_D = 3 * PAIRS
R_OF_D = 4 * PAIRS
N_RAW = D_END + R_OF_D
GAIN_ROWS = PAIRS + (D_END - D_OUT) // 2


def n_tiles(u):
    return min(u + 1, 5) if u < SAMPLE_UNIT else 5


def unit_no(j, u):
    return UNITS * j + u + 1


def head_no(j, u, h):
    return (2 * UNITS - 1) * j + 2 * u + h + 1


def turned_no(j, u):
    return 15 * j + (u + 1 if u < 3 else 3 + 2 * (u - 2))


def second_no(j, u):
    return SAMPLE_UNIT * j + min(u, SAMPLE_UNIT - 1) + 1


def block_no(j, c):
    return BLOCKS * j + c + 1


HIGH_COPIES = (4, 1, 2)


def high_no(j, c, n):
    return 21 * j + 7 * (c // 3) + sum(HIGH_COPIES[:c % 3]) + n + 1


def build(nc, x_t, p_t, w_stream, w_ple, gains, vecs, w_pool, state_t, bias_ext,
          y_t, k_new, v_new, pool_p, pool_s):
    bias_rows = nc.dram_tensor("bias_rows", (N_HEADS, P, WIN), F32, kind="Internal").ap()

    TILE = TOK * 4
    ACTS = KT * TILE
    base = 16512

    def at(name, shape, off, dt=F32):
        return nc.alloc_sbuf_tensor_at(name, [P] + shape, dt, offset=base + off)

    o_xh, o_xl, o_mh, o_ml, o_y = (i * ACTS for i in range(5))
    o_w = 5 * ACTS
    o_rb = o_w + 6 * 4096
    o_ss = o_rb + TILE
    o_tb = o_ss + TILE
    o_const = o_tb + 4 * 1536

    xh = at("xh", [KT, TOK], o_xh, F32R)
    xl = at("xl", [KT, TOK], o_xl, F32R)
    xsum = at("xsum", [KT, TOK], o_xl)
    mh = at("mh", [KT, TOK], o_mh, F32R)
    ml = at("ml", [KT, TOK], o_ml, F32R)
    mix = at("mix", [KT, TOK], o_ml)
    xsq = at("xsq", [KT, TOK], o_ml)
    y = at("y", [KT, TOK], o_y)

    w_raw = [at(f"w_raw{s}", [KT, P], o_w + s * 4096) for s in range(2)]
    wh = [at(f"wh{s}", [KT, P], o_w + (2 + s) * 4096, F32R) for s in range(2)]
    wl = [at(f"wl{s}", [KT, P], o_w + (4 + s) * 4096, F32R) for s in range(2)]
    rb = at("rb", [TOK], o_rb)
    ss = at("ss", [TOK], o_ss)
    tb = at("tb", [4, 384], o_tb)
    tmp = at("tmp", [TOK], o_tb)
    pool_w = at("pool_w", [GROUPS, P], o_tb)

    ones = at("ones", [P], o_const)
    ident = at("ident", [P], o_const + 512)
    gain = at("gain", [GAIN_ROWS, KT], o_const + 1024)
    vec = at("vec", [4, KT], o_const + 2432)
    state = at("state", [GROUPS, HIST], o_const + 2560)
    inv_n = at("inv_n", [16], o_const + 2816)
    neg_max = at("neg_max", [2], o_const + 2880)
    row_sum = at("row_sum", [2], o_const + 2912)
    inv_sum = at("inv_sum", [2], o_const + 2944)

    q_h = [at(f"q_h{h}", [2, 384], o_mh + h * 3072, F32R) for h in range(2)]
    q_l = [at(f"q_l{h}", [2, 384], o_mh + (2 + h) * 3072, F32R) for h in range(2)]
    kk = [at(f"kk{h}", [TOK], o_mh + 12288 + h * TILE, F32R) for h in range(2)]
    v_h = at("v_h", [9, P], o_mh + 20736, F32R)
    v_l = at("v_l", [9, P], o_mh + 25344, F32R)
    q_s = at("q_s", [2, 2, 64], o_mh + 29952, F32R)
    bias_s = at("bias_s", [SKEYS], o_mh + 30976)
    pt_h = at("pt_h", [5, 256], o_y, F32R)
    pt_l = at("pt_l", [5, 256], o_y + 5120, F32R)
    prob = at("prob", [2, WIN], o_y + 10240)
    vc_h = at("vc_h", [4, P], o_y + 15360, F32R)
    vc_l = at("vc_l", [4, P], o_y + 17408, F32R)
    bias = at("bias", [2, WIN], o_y + 19456)
    kc = [at(f"kc{h}", [CACHE], o_y + 24576 + h * 2048, F32R) for h in range(2)]
    wh3 = at("wh3", [KT, P], o_ss, F32R)
    wl3 = at("wl3", [KT, P], o_y + 28672, F32R)
    a_wh, a_wl = (wh[0], wh[1], wh3), (wl[0], wl[1], wl3)
    neg = at("neg", [CHUNK], o_mh)
    u_ext = at("u_ext", [UCOLS], o_y)
    run_sum = [at("run_sum0", [UCOLS], o_y + 4352), at("run_sum1", [UCOLS], o_y + 8704)]
    diff = at("diff", [TOK], o_y + 13056)
    p_h = at("p_h", [2, TOK], o_mh, F32R)
    p_l = at("p_l", [2, TOK], o_mh + 2 * TILE, F32R)
    wp_h = [at(f"wp_h{s}", [2, P], o_mh + 4 * TILE + s * 1024, F32R) for s in range(2)]
    wp_l = [at(f"wp_l{s}", [2, P], o_mh + 4 * TILE + 2048 + s * 1024, F32R) for s in range(2)]
    wp_raw = at("wp_raw", [KT, 2, P], o_mh + 4 * TILE + 4096)
    p_raw = at("p_raw", [2, TOK], o_ml)
    xsum2 = at("xsum2", [KT, TOK], o_ml)

    with ExitStack() as ctx:
        ps = ctx.enter_context(nc.psum_tensor("ps", [P, 8, 512], F32))
        flat = ps[:, :, :].rearrange("p a b -> p (a b)")

        def dense_ps(s):
            return ps[:, NB * s:NB * s + NB, 0:BW]

        def blocks(t):
            return t.rearrange("p (a b) -> p a b", a=NB)

        def score_cols(h):
            return 2 * 512 + (128 if h == 0 else 768)

        SAMPLE_COL = 2 * 512
        pv_ps = flat[:, 5 * 512:5 * 512 + 256]
        turned = flat[:, 5 * 512 + 256:8 * 512].rearrange("p (t c) -> p t c", c=256)

        def parts(n):
            return ((0, min(n, 3)),) if n <= 3 else ((0, 3), (3, n))

        def sem(name):
            return ctx.enter_context(nc.semaphore(name))

        x_in = [sem(f"x_in{k}") for k in range(KT)]
        raw_in = [sem("raw_in0"), sem("raw_in1")]
        vecs_in, pool_w_in, state_in, gains_in = sem("vecs_in"), sem("pool_w_in"), sem("state_in"), sem("gains_in")
        rows_in, corners_in, bias_in, bias_s_in = sem("rows_in"), sem("corners_in"), sem("bias_in"), sem("bias_s_in")
        p_in, wp_in = sem("p_in"), sem("wp_in")
        k_out, v_out, u_out, y_out = sem("k_out"), sem("v_out"), sem("u_out"), sem("y_out")
        const_made = sem("const_made")
        w_gained, w_high, w_low = sem("w_gained"), sem("w_high"), sem("w_low")
        x_high, x_low, x_sq = sem("x_high"), sem("x_low"), sem("x_sq")
        stat_mm, stat_var, stat_root, stat_inv = sem("stat_mm"), sem("stat_var"), sem("stat_root"), sem("stat_inv")
        tile_mm, tile_out = sem("tile_mm"), sem("tile_out")
        u_run, u_diff, pool_mm, pool_put = sem("u_run"), sem("u_diff"), sem("pool_mm"), sem("pool_put")
        blk_mm, blk_t, blk_high, blk_low, v_turn = sem("blk_mm"), sem("blk_t"), sem("blk_high"), sem("blk_low"), sem("v_turn")
        q_dup = sem("q_dup")
        qs_zero, qs_put = sem("qs_zero"), sem("qs_put")
        s_mm, s_max, s_exp = sem("s_mm"), sem("s_max"), sem("s_exp")
        s_inv = [sem("s_inv0"), sem("s_inv1")]
        s_norm = [sem("s_norm0"), sem("s_norm1")]
        t_mm, t_high, t_low, pv_mm, mix_put = sem("t_mm"), sem("t_high"), sem("t_low"), sem("pv_mm"), sem("mix_put")
        mix_high, mix_low = sem("mix_high"), sem("mix_low")
        sq_put, sq_sum = sem("sq_put"), sem("sq_sum")
        scaled, added, xsum_put = sem("scaled"), sem("added"), sem("xsum_put")
        sq_done, hid_high, hid_low = sem("sq_done"), sem("hid_high"), sem("hid_low")
        p_high, p_low, wp_high, wp_low = sem("p_high"), sem("p_low"), sem("wp_high"), sem("wp_low")
        ple_mm, gate_put, gated, zeroed, carried = sem("ple_mm"), sem("gate_put"), sem("gated"), sem("zeroed"), sem("carried")

        block = ctx.enter_context(nc.Block())

        def apart(eng):
            eng.sem_inc(carried, 1)

        SLOT_UNITS = [(-1, 6), (-1, 7), (-1, 8), (0, 0), (0, 1), (0, 2), (0, 3), (0, 4), (0, 5)]

        def attention(eng, slot):
            def run(j, first):
                for c in range(BLOCKS):
                    dj, u = SLOT_UNITS[c]
                    unit = None if first and dj < 0 else (j + dj, u)
                    up = (u - 1) % UNITS
                    prev = None if first and c <= 3 else (j + dj - (1 if u == 0 else 0), up)
                    slot(j, c, unit, prev)
            run(0, True)
            with eng.Fori(1, PAIRS) as j:
                run(j, False)
            last = PAIRS - 1
            slot(PAIRS, None, (last, 6), (last, 5))
            slot(PAIRS, None, (last, 7), (last, 6))
            slot(PAIRS, None, (last, 8), (last, 7))
            slot(PAIRS, None, None, (last, 8))

        @block.sync
        def _(sp):
            def load_raw(r, s):
                sp.dma_start(w_raw[s][:, :, :], w_stream[bass.ds(r, 1)].rearrange("a p (k n) -> p (a k) n", k=KT))\
                  .then_inc(raw_in[s], 16)

            def next_raw(r, s):
                sp.wait_ge(w_low, r - 1)
                load_raw(r, s)

            def load_bias(j):
                sp.dma_start(bias[:, :, :], bias_rows[bass.ds(2 * j, 2)].rearrange("h p c -> p h c"))\
                  .then_inc(bias_in, 16)

            def load_bias_s(j):
                for h in range(2):
                    sp.dma_start(bias_s[DEC * h:DEC * h + DEC, :],
                                 bias_rows[bass.ds(2 * j + h, 1), 0:DEC, 0:SKEYS].rearrange("a p c -> (a p) c"))\
                      .then_inc(bias_s_in, 16)

            load_raw(0, 0)
            for k in range(KT):
                sp.dma_start(y[:, k, :], x_t[k]).then_inc(x_in[k], 16)
                if k == 1:
                    load_raw(1, 1)
            sp.wait_ge(rows_in, 16)
            sp.wait_ge(const_made, 4)
            rows = bias_rows.rearrange("h p c -> p h c")
            for h in range(N_HEADS):
                sp.dma_start(rows[0:CHUNK, h, WIN - CHUNK:WIN], neg[0:CHUNK, :]).then_inc(corners_in, 16)
                sp.dma_start(rows[CHUNK:P, h, 0:CHUNK], neg[CHUNK:P, :]).then_inc(corners_in, 16)
            next_raw(2, 0)
            next_raw(3, 1)
            sp.wait_ge(corners_in, 16 * 2 * N_HEADS)
            sp.wait_ge(x_low, KT)
            sp.wait_ge(x_sq, KT)
            load_bias(0)
            load_bias_s(0)
            for i in range(4):
                next_raw(W_U + i, i % 2)
            with sp.Fori(1, PAIRS) as j:
                for i in range(4):
                    next_raw(4 * j + W_U + i, i % 2)
                sp.wait_ge(s_max, head_no(j - 1, 7, 1))
                load_bias(j)
                sp.wait_ge(s_max, head_no(j - 1, 8, 0))
                load_bias_s(j)
            with sp.Fori(0, (N_RAW - 4 * PAIRS - W_U) // 2) as i:
                for s in range(2):
                    next_raw(2 * i + (4 * PAIRS + W_U + s), s)
            for k in range(KT):
                sp.wait_ge(added, 2 * KT + k + 1)
                sp.dma_start(y_t[k], y[:, k, :]).then_inc(y_out, 16)
            sp.wait_ge(y_out, 16 * KT)
            sp.wait_ge(u_out, 16 * 2 * GROUPS)
            sp.wait_ge(k_out, 16 * 2 * PAIRS)
            sp.wait_ge(v_out, 16 * 2 * PAIRS)

        @block.tensor
        def _(pe):
            def split3(out, w_hi, w_lo, a_hi, a_lo, first, last):
                pe.matmul(out, w_hi, a_hi, start=first, stop=False)
                pe.matmul(out, w_hi, a_lo, start=False, stop=False)
                return pe.matmul(out, w_lo, a_hi, start=False, stop=last)

            def dense_k(s, k, a_hi, a_lo):
                for b in range(NB):
                    mm = split3(ps[:, NB * s + b, 0:BW], wh[s][:, k, :], wl[s][:, k, :],
                                a_hi[:, k, b * BW:(b + 1) * BW], a_lo[:, k, b * BW:(b + 1) * BW],
                                k == 0, k == KT - 1)
                return mm

            def weights_ready(r):
                pe.wait_ge(w_high, r + 1)
                pe.wait_ge(w_low, r + 1)

            def dense_tile(d, s, a_hi, a_lo):
                weights_ready(d + R_OF_D)
                pe.wait_ge(tile_out, d - 1)
                for k in range(KT):
                    mm = dense_k(s, k, a_hi, a_lo)
                mm.then_inc(tile_mm, 1)

            def first_tile(r, d_free, stage, stats):
                weights_ready(r)
                if d_free:
                    pe.wait_ge(tile_out, d_free)
                for k in range(KT):
                    pe.wait_ge(x_high, KT * stage + k + 1)
                    pe.wait_ge(x_low, KT * stage + k + 1)
                    mm = dense_k(0, k, xh, xl)
                    if k == KT - 1:
                        mm.then_inc(tile_mm, 1)
                    if stats:
                        pe.wait_ge(x_sq, KT * stage + k + 1)
                        for b in range(NB):
                            mm = pe.matmul(ps[:, NB + b, 0:BW], ones[:, :], xsq[:, k, b * BW:(b + 1) * BW],
                                           start=(k == 0), stop=(k == KT - 1))
                        if k == KT - 1:
                            mm.then_inc(stat_mm, 1)

            def out_stats(n):
                pe.wait_ge(sq_sum, KT * n + 1)
                for b in range(NB):
                    mm = pe.matmul(ps[:, b, 0:BW], ones[:, :], ss[:, b * BW:(b + 1) * BW], start=True, stop=True)
                mm.then_inc(stat_mm, 1)

            pe.wait_ge(const_made, 4)
            first_tile(0, 0, 0, True)

            def u_tile(g):
                weights_ready(g)
                if g == 1:
                    pe.wait_ge(stat_var, 1)
                if g >= 2:
                    pe.wait_ge(pool_put, g - 1)
                for k in range(KT):
                    mm = dense_k(g % 2, k, xh, xl)
                mm.then_inc(tile_mm, 1)

            def pool_tile(g):
                if g == 0:
                    pe.wait_ge(pool_w_in, 16)
                pe.wait_ge(u_diff, g + 1)
                for b in range(NB):
                    mm = pe.matmul(ps[:, NB * (g % 2) + b, 0:BW], pool_w[:, g, :], diff[:, b * BW:(b + 1) * BW],
                                   start=True, stop=True)
                mm.then_inc(pool_mm, 1)

            u_tile(1)
            pool_tile(0)
            u_tile(2)
            pool_tile(1)
            u_tile(3)
            pool_tile(2)
            pool_tile(3)

            def proj(j, c, half):
                t, (tok, n) = c % 3, ABLK[c // 3]
                out = ps[:, c % 2, 0:n]
                if half == 0:
                    if c < 3:
                        weights_ready(4 * j + W_U + t)
                    if not isinstance(j, int) or j > 0 or c >= 2:
                        before = c - 2 if c else -1
                        if before % 3 == V:
                            pe.wait_ge(blk_low, block_no(j, before if c > 1 else -2))
                        else:
                            pe.wait_ge(blk_t, block_no(j, before if c > 1 else -1 - c))
                for k in range(4 * half, 4 * half + 4):
                    mm = split3(out, a_wh[t][:, k, :], a_wl[t][:, k, :], xh[:, k, tok:tok + n], xl[:, k, tok:tok + n],
                                k == 0, k == KT - 1)
                if half:
                    mm.then_inc(blk_mm, 1)

            def turn_v(j, c):
                tok, n = ABLK[c // 3]
                pe.wait_ge(blk_t, block_no(j, c))
                for i in range(0, n, P):
                    m = min(P, n - i)
                    mm = pe.transpose(ps[0:m, c % 2, i:i + P], tb[:, 1, i:i + m], ident[:, :])
                mm.then_inc(v_turn, 1)

            def scores(j, u):
                if u < SAMPLE_UNIT:
                    b, n = u // 3, n_tiles(u)
                    pe.wait_ge(blk_low, block_no(j, 3 * b + K))
                    pe.wait_ge(blk_high, high_no(j, 3 * b + K, 1))
                    pe.wait_ge(q_dup, 6 * j + 2 * b + 2)
                    if isinstance(j, int) and j == 0 and u == 0:
                        pe.wait_ge(pool_put, GROUPS)
                    else:
                        pe.wait_ge(s_max, head_no(j, u - 1, 1))
                    lo = WIN - P * n
                    q0 = P * u - ABLK[b][0]
                    cuts = ((0, max(lo, 384), WIN), (1, lo, 256), (0, lo, 384), (1, max(lo, 256), WIN))
                    for i, (h, a, e) in enumerate(cuts):
                        if e > a:
                            out = flat[:, score_cols(h) + a:score_cols(h) + e]
                            key0 = P * (u + 1) - WIN + a
                            keys = kk[h][:, key0:key0 + e - a]
                            pe.matmul(out, q_h[h][:, b % 2, q0:q0 + P], keys, start=True, stop=False)
                            mm = pe.matmul(out, q_l[h][:, b % 2, q0:q0 + P], keys, start=False, stop=True)
                        if i >= 2:
                            mm.then_inc(s_mm, 1)
                else:
                    pe.wait_ge(qs_put, 4 * j + 4)
                    pe.wait_ge(s_max, head_no(j, u - 1, 1))
                    pe.wait_ge(w_low, 4 * j + W_U + 4)
                    for a, e in ((0, CACHE), (CACHE, SKEYS)):
                        out = flat[0:64, SAMPLE_COL + a:SAMPLE_COL + e]
                        for i in range(4):
                            h = i // 2
                            keys = kc[h][:, :] if a < CACHE else kk[h][:, SEQ:TOK]
                            mm = pe.matmul(out, q_s[:, i % 2, h, :], keys, start=(i == 0), stop=(i == 3))
                    mm.then_inc(s_mm, 1)

            def turn(j, u):
                n = n_tiles(u)
                whole = u < SAMPLE_UNIT
                pe.wait_ge(s_norm[0], unit_no(j, u))
                if u > 0 or not isinstance(j, int) or j > 0:
                    pe.wait_ge(t_low, turned_no(j, u - 1) if u > 0 else turned_no(j - 1, 8))
                    pe.wait_ge(mix_put, unit_no(j, u - 1))
                if not whole:
                    apart(pe)
                for i0, i1 in parts(n):
                    if whole:
                        for h in range(2):
                            if h == 1 and i0 == 0:
                                pe.wait_ge(s_norm[1], second_no(j, u))
                            for i in range(i0, i1):
                                c0 = WIN - P * n + P * i
                                mm = pe.transpose(turned[:, i, P * h:P * h + P], prob[:, h, c0:c0 + P], ident[:, :])
                    else:
                        for i in range(i0, i1):
                            m = P if i < 4 else DEC
                            mm = pe.transpose(turned[0:m, i, 0:64], prob[0:64, 0, P * i:P * i + m], ident[0:64, 0:64])
                    mm.then_inc(t_mm, 1)

            def weigh_values(j, u):
                n = n_tiles(u)
                pe.wait_ge(t_low, turned_no(j, u) - (len(parts(n)) - 1))
                whole = u < SAMPLE_UNIT
                pe.wait_ge(blk_low, block_no(j, 3 * (u // 3 if whole else 2) + V))
                cols = 256
                for i in range(n):
                    rows = P
                    if i == 3:
                        pe.wait_ge(t_low, turned_no(j, u))
                    if whole:
                        t = u + 1 - n + i
                        vh, vl = v_h[:, t, :], v_l[:, t, :]
                    elif i < 4:
                        vh, vl = vc_h[:, i, :], vc_l[:, i, :]
                    else:
                        rows = DEC
                        vh, vl = v_h[0:DEC, 8, :], v_l[0:DEC, 8, :]
                    mm = split3(pv_ps[:, 0:cols], vh, vl, pt_h[0:rows, i, 0:cols], pt_l[0:rows, i, 0:cols],
                                i == 0, i == n - 1)
                mm.then_inc(pv_mm, 1)

            def slot(j, c, unit, prev):
                if c is not None:
                    if isinstance(j, int) and j == 0 and c == 0:
                        pe.wait_ge(pool_put, GROUPS - 1)
                    proj(j, c, 0)
                if c is not None and c % 3 == 2:
                    turn_v(j, c - 1)
                if unit:
                    scores(*unit)
                if prev:
                    weigh_values(*prev)
                if c is not None:
                    proj(j, c, 1)
                if unit:
                    turn(*unit)

            attention(pe, slot)

            def out_tile(d, s, first):
                weights_ready(d + R_OF_D)
                pe.wait_ge(tile_out, d - 1)
                for k in range(KT):
                    if first:
                        pe.wait_ge(mix_high, k + 1)
                        pe.wait_ge(mix_low, k + 1)
                    mm = dense_k(s, k, mh, ml)
                mm.then_inc(tile_mm, 1)

            pe.wait_ge(blk_low, block_no(PAIRS - 1, BLOCKS - 1))
            pe.wait_ge(pool_put, GROUPS)
            pe.wait_ge(s_max, head_no(PAIRS - 1, 8, 0))
            pe.wait_ge(t_low, turned_no(PAIRS - 1, 8))
            out_tile(D_OUT, 0, True)
            out_tile(D_OUT + 1, 1, False)
            with pe.Fori(1, KT // 2) as i:
                for s in range(2):
                    dense_tile(2 * i + (D_OUT + s), s, mh, ml)
            pe.wait_ge(tile_out, D_FF - 1)
            out_stats(1)

            pe.wait_ge(tile_out, D_FF)
            pe.wait_ge(stat_var, 2)
            first_tile(D_FF + R_OF_D, 0, 1, True)
            pe.wait_ge(stat_var, 3)
            dense_tile(D_FF + 1, 1, xh, xl)
            with pe.Fori(1, KT // 2) as i:
                for s in range(2):
                    dense_tile(2 * i + (D_FF + s), s, xh, xl)

            def second(c):
                d = 2 * KT * c + (D_FF + KT)
                weights_ready(d + R_OF_D)
                pe.wait_ge(tile_out, d - 1)
                for k in range(KT):
                    if k >= KT - 2:
                        pe.wait_ge(hid_low, KT * c + k + 1)
                    mm = dense_k(0, k, mh, ml)
                mm.then_inc(tile_mm, 1)
                dense_tile(d + 1, 1, mh, ml)
                with pe.Fori(1, KT // 2) as i:
                    for s in range(2):
                        dense_tile(2 * KT * c + 2 * i + (D_FF + KT + s), s, mh, ml)

            second(0)
            with pe.Fori(1, FF_CHUNKS) as c:
                with pe.Fori(0, KT // 2) as i:
                    for s in range(2):
                        dense_tile(2 * KT * c + 2 * i + (D_FF + s), s, xh, xl)
                second(c)
            pe.wait_ge(tile_out, D_GATE - 1)
            out_stats(2)

            def ple_tile(m, s, first=False):
                d = m + D_GATE
                if first:
                    pe.wait_ge(stat_var, 4)
                    first_tile(D_GATE + R_OF_D, 0, 2, False)
                else:
                    weights_ready(d + R_OF_D)
                    pe.wait_ge(gate_put, m)
                    for k in range(KT):
                        for b in range(NB):
                            mm = split3(ps[:, b, 0:BW], wh[s][:, k, :], wl[s][:, k, :],
                                        xh[:, k, b * BW:(b + 1) * BW], xl[:, k, b * BW:(b + 1) * BW],
                                        k == 0, k == KT - 1)
                    mm.then_inc(tile_mm, 1)
                if first:
                    pe.wait_ge(tile_out, D_GATE)
                    pe.wait_ge(p_low, 1)
                else:
                    pe.wait_ge(gated, m)
                pe.wait_ge(wp_low, m + 1)
                for k in range(2):
                    for b in range(NB):
                        mm = split3(ps[:, NB + b, 0:BW], wp_h[s][:, k, :], wp_l[s][:, k, :],
                                    p_h[:, k, b * BW:(b + 1) * BW], p_l[:, k, b * BW:(b + 1) * BW],
                                    k == 0, k == 1)
                mm.then_inc(ple_mm, 1)

            ple_tile(0, 0, True)
            ple_tile(1, 1)
            with pe.Fori(1, KT // 2) as i:
                for s in range(2):
                    ple_tile(2 * i + s, s)
            pe.wait_ge(gate_put, KT)
            out_stats(3)

        @block.scalar
        def _(act):
            def act_copy(out, in_):
                return act.activation(out, in_, ACT.Copy)

            def split_high(w, r, s, hi):
                act.wait_ge(w_gained, w + 1)
                act_copy(hi[:, :, :], w_raw[s][:, :, :]).then_inc(w_high, 1)

            def ahead(d, s):
                act.wait_ge(tile_mm, d + 1)
                split_high(d + 2 + W_OF_D, d + 2 + R_OF_D, s, wh[s])

            act.dma_start(gain[:, :, :], gains).then_inc(gains_in, 16)
            act.dma_start(vec[:, :, :], vecs).then_inc(vecs_in, 16)
            src = bass.AP(bias_ext.tensor, P - 1, [[EXT, N_HEADS], [-1, P], [1, WIN]])
            act.dma_start(bias_rows, src).then_inc(rows_in, 16)
            act.dma_start(pool_w[:, :, :], w_pool).then_inc(pool_w_in, 16)
            act.dma_start(state[:, :, :], state_t).then_inc(state_in, 16)

            def x_parts(stage, k, squares):
                act_copy(xh[:, k, :], y[:, k, :]).then_inc(x_high, 1)
                if squares:
                    act.activation(xsq[:, k, :], y[:, k, :], ACT.Square).then_inc(x_sq, 1)

            def root(n, t):
                act.wait_ge(stat_var, n)
                act.activation(t[:, :], t[:, :], ACT.Sqrt).then_inc(stat_root, 1)

            for k in range(KT):
                act.wait_ge(x_in[k], 16)
                x_parts(0, k, True)
                if k < 2:
                    split_high(k, k, k, wh[k])
            root(1, rb)

            for g in range(GROUPS):
                act.wait_ge(tile_mm, g + 1)
                split_high(g + 2, g + 2, g % 2, wh[g % 2])
                act.wait_ge(tile_out, g + 1)
                act.dma_start(pool_p[g], u_ext[:, SEQ:SEQ + HIST]).then_inc(u_out, 16)
                act.dma_start(pool_s[g], u_ext[:, UCOLS - HIST:UCOLS]).then_inc(u_out, 16)
                if g == 0:
                    act.wait_ge(vecs_in, 16)
                if g == GROUPS - 1:
                    split_high(W_U + 2, W_U + 2, 0, wh3)
                if g >= 1:
                    act.wait_ge(pool_mm, g)
                    act.activation(mix[:, GROUPS + g - 1, :].rearrange("p (a b) -> p a b", a=NB), dense_ps((g - 1) % 2),
                                   ACT.Identity, scale=vec[:, 3, g - 1:g]).then_inc(pool_put, 1)
            act.wait_ge(pool_mm, GROUPS)
            act.activation(mix[:, 2 * GROUPS - 1, :].rearrange("p (a b) -> p a b", a=NB), dense_ps(1),
                           ACT.Identity, scale=vec[:, 3, GROUPS - 1:GROUPS]).then_inc(pool_put, 1)

            def block_high(j, c):
                t, b = c % 3, c // 3
                tok, n = ABLK[b]
                if t == V:
                    return
                act.wait_ge(blk_t, block_no(j, c))
                if t == K:
                    for h in range(2):
                        r = slice(64 * h, 64 * h + 64)
                        act_copy(kk[h][r, tok:tok + n], tb[r, K, 0:n]).then_inc(blk_high, 1)
                else:
                    for dup in range(2):
                        for h in range(2):
                            r = slice(64 * h, 64 * h + 64)
                            o = r if dup == 0 else slice(64 - 64 * h, 128 - 64 * h)
                            act_copy(q_h[h][o, b % 2, 0:n], tb[r, Q, 0:n]).then_inc(blk_high, 1)

            def store_block(j, c):
                t, b = c % 3, c // 3
                if t == Q or b == 0:
                    return
                act.wait_ge(blk_t, block_no(j, c))
                n0, o0 = (P, 0) if b == 1 else (0, 2 * P)
                new, stored = (k_new, k_out) if t == K else (v_new, v_out)
                act.dma_start(new[bass.ds(j, 1), :, o0:o0 + ABLK[b][1] - n0].rearrange("a p c -> (a p) c"),
                              tb[:, t, n0:ABLK[b][1]]).then_inc(stored, 16)

            def v_high(j, c):
                b = c // 3
                act.wait_ge(v_turn, 3 * j + b + 1)
                if b < 2:
                    act_copy(v_h[:, 3 * b:3 * b + 3, :],
                             ps[:, c % 2, 0:384].rearrange("p (t d) -> p t d", d=P)).then_inc(blk_high, 1)
                else:
                    act_copy(v_h[:, 6:8, :], ps[:, c % 2, 0:256].rearrange("p (t d) -> p t d", d=P))
                    act_copy(v_h[0:DEC, 8, :], ps[0:DEC, c % 2, 256:384]).then_inc(blk_high, 1)

            def turned_high(j, u):
                cols = 256 if u < SAMPLE_UNIT else 64
                p = parts(n_tiles(u))
                for n, (i0, i1) in enumerate(p):
                    act.wait_ge(t_mm, turned_no(j, u) - (len(p) - 1 - n))
                    act_copy(pt_h[:, i0:i1, 0:cols], turned[:, i0:i1, 0:cols]).then_inc(t_high, 1)

            def exps(j, u):
                if u < SAMPLE_UNIT:
                    lo = WIN - P * n_tiles(u)
                    for h in range(2):
                        act.wait_ge(s_max, head_no(j, u, h))
                        act.activation(prob[:, h, lo:WIN], prob[:, h, lo:WIN], ACT.Exp, scale=-1.0,
                                       bias=neg_max[:, h:h + 1], accum_out=row_sum[:, h:h + 1]).then_inc(s_exp, 1)
                else:
                    act.wait_ge(s_max, head_no(j, u, 0))
                    act.activation(prob[0:64, 0, 0:SKEYS], prob[0:64, 0, 0:SKEYS], ACT.Exp, scale=-1.0,
                                   bias=neg_max[0:64, 0:1], accum_out=row_sum[0:64, 0:1]).then_inc(s_exp, 1)

            def put_mix(j, u):
                act.wait_ge(pv_mm, unit_no(j, u))
                tok, n = P * u, (P if u < SAMPLE_UNIT else DEC)
                for h in range(2):
                    r = slice(64 * h, 64 * h + 64)
                    i = act_copy(mix[r, bass.ds(j, 1), tok:tok + n], pv_ps[r, n * h:n * h + n].rearrange("p (a c) -> p a c", a=1))
                i.then_inc(mix_put, 1)

            def split_cache(j):
                r = 4 * j + W_U + 3
                act.wait_ge(raw_in[1], 16 * (2 * j + 4))
                if not isinstance(j, int) or j > 0:
                    act.wait_ge(pv_mm, UNITS * j)
                raw = w_raw[1][:, :, :].rearrange("p k n -> p (k n)")
                for h in range(2):
                    rr = slice(64 * h, 64 * h + 64)
                    act_copy(kc[h][rr, :], raw[rr, 0:CACHE])
                act_copy(vc_h[:, :, :], raw[:, CACHE:2 * CACHE].rearrange("p (t d) -> p t d", d=P)).then_inc(w_high, 1)

            def slot(j, c, unit, prev):
                if c is not None:
                    if c == 0 and not (isinstance(j, int) and j == 0):
                        block_high(j - 1, 8)
                    if c > 0 and (c - 1) % 3 != Q:
                        block_high(j, c - 1)
                elif unit and unit[1] == 6:
                    block_high(j - 1, 8)
                if prev:
                    turned_high(*prev)
                if c is not None and c % 3 == 2:
                    v_high(j, c - 1)
                if unit:
                    exps(*unit)
                if prev:
                    put_mix(*prev)
                if c is not None and c % 3 == 1:
                    block_high(j, c - 1)
                if c == 3:
                    split_cache(j)
                if c is not None and c > 0:
                    store_block(j, c - 1)
                elif c == 0 and not (isinstance(j, int) and j == 0) or c is None and unit and unit[1] == 6:
                    store_block(j - 1, 8)
                if c is not None:
                    if c == 0 and not (isinstance(j, int) and j == 0):
                        act.wait_ge(blk_mm, block_no(j - 1, 8))
                        split_high(3 * j + W_U + 2, 0, 0, wh3)
                    if c == 7:
                        act.wait_ge(blk_mm, block_no(j, 6))
                        split_high(3 * j + W_U + 3, 0, 0, wh[0])
                    if c == 8:
                        act.wait_ge(blk_mm, block_no(j, 7))
                        split_high(3 * j + W_U + 4, 0, 1, wh[1])

            act.wait_ge(corners_in, 16 * 2 * N_HEADS)
            act.wait_ge(u_out, 16 * 2 * GROUPS)
            attention(act, slot)

            act.wait_ge(mix_put, UNITS * PAIRS)
            act.wait_ge(pool_put, GROUPS)
            act.wait_ge(k_out, 32 * PAIRS)
            act.wait_ge(v_out, 32 * PAIRS)
            for k in range(KT):
                act_copy(mh[:, k, :], mix[:, k, :]).then_inc(mix_high, 1)

            def out_step(d, s):
                ahead(d, s)
                m = d - D_OUT
                act_copy(blocks(y[:, bass.ds(m, 1), :].rearrange("p a t -> p (a t)")), dense_ps(s))
                act.wait_ge(sq_sum, m + 1)
                act.activation(blocks(tmp[:, :]), dense_ps(s), ACT.Square).then_inc(tile_out, 1)

            with act.Fori(0, KT // 2) as i:
                for s in range(2):
                    out_step(2 * i + (D_OUT + s), s)
            root(2, ss)

            def new_x(stage, squares):
                for k in range(KT):
                    act.wait_ge(added, KT * (stage - 1) + k + 1)
                    x_parts(stage, k, squares)

            new_x(1, True)
            root(3, rb)

            def hidden_step(d, s, n, m):
                ahead(d, s)
                act.wait_ge(tile_out, d + 1)
                act.activation(tmp[:, :], tmp[:, :], ACT.Square).then_inc(sq_done, 1)
                act.wait_ge(sq_done, n + 1)
                act_copy(mh[:, bass.ds(m, 1), :].rearrange("p a t -> p (a t)"), tmp[:, :]).then_inc(hid_high, 1)

            def ff_chunk(c, last):
                with act.Fori(0, KT // 2) as i:
                    for s in range(2):
                        hidden_step(2 * KT * c + 2 * i + (D_FF + s), s, KT * c + 2 * i + s, 2 * i + s)
                with act.Fori(0, KT // 2) as i:
                    for s in range(2):
                        d = 2 * KT * c + 2 * i + (D_FF + KT + s)
                        ahead(d, s)
                        if last:
                            m = 2 * i + s
                            act.wait_ge(tile_out, d + 1)
                            act.wait_ge(sq_sum, m + (KT + 1))
                            act.wait_ge(hid_low, KT * FF_CHUNKS)
                            act.activation(tmp[:, :], y[:, bass.ds(m, 1), :].rearrange("p a t -> p (a t)"), ACT.Square)\
                               .then_inc(sq_put, 1)

            with act.Fori(0, FF_CHUNKS - 1) as c:
                ff_chunk(c, False)
            ff_chunk(FF_CHUNKS - 1, True)

            act.wait_ge(tile_mm, D_GATE)
            act.dma_start(p_raw[:, :, :], p_t).then_inc(p_in, 16)
            act.dma_start(wp_raw[:, :, :, :], w_ple).then_inc(wp_in, 16)
            root(4, ss)
            new_x(2, False)
            act.wait_ge(p_in, 16)
            act_copy(p_h[:, :, :], p_raw[:, :, :]).then_inc(p_high, 1)
            act.wait_ge(wp_in, 16)

            def split_wp(m, s):
                act_copy(wp_h[s][:, :, :], wp_raw[:, bass.ds(m, 1), :, :].rearrange("p a k n -> p (a k) n"))\
                    .then_inc(wp_high, 1)

            split_wp(0, 0)
            split_wp(1, 1)

            def gate_step(m, s, more):
                act.wait_ge(tile_mm, m + D_GATE + 1)
                if more:
                    split_high(m + (D_GATE + 2 + W_OF_D), 0, s, wh[s])
                act.wait_ge(sq_sum, m + (2 * KT + 1))
                act.activation(blocks(tmp[:, :]), dense_ps(0), ACT.Sigmoid).then_inc(gate_put, 1)
                act.wait_ge(gated, m + 1)
                act.activation(tmp[:, :], y[:, bass.ds(m, 1), :].rearrange("p a t -> p (a t)"), ACT.Square)\
                   .then_inc(sq_put, 1)
                if more:
                    split_wp(m + 2, s)

            with act.Fori(0, KT // 2 - 1) as i:
                for s in range(2):
                    gate_step(2 * i + s, s, True)
            for s in range(2):
                gate_step(KT - 2 + s, s, False)
            root(5, ss)

        @block.vector
        def _(dve):
            def sub(out, a, b):
                return dve.tensor_tensor(out, a, b, ALU.subtract)

            def split_low(r, s, hi, lo):
                dve.wait_ge(w_high, r + 1)
                sub(lo[:, :, :], w_raw[s][:, :, :], hi[:, :, :]).then_inc(w_low, 1)

            def ahead(d, s):
                dve.wait_ge(tile_mm, d + 1)
                split_low(d + 2 + R_OF_D, s, wh[s], wl[s])

            def variance(n, t, src):
                dve.wait_ge(stat_mm, n)
                dve.tensor_scalar(blocks(t[:, :]), src, 1.0 / D_MODEL, EPS, ALU.mult, ALU.add).then_inc(stat_var, 1)

            def inverse(n, t):
                dve.wait_ge(stat_root, n)
                dve.reciprocal(t[:, :], t[:, :]).then_inc(stat_inv, 1)
                dve.wait_ge(stat_inv, n)

            for k in range(KT):
                dve.wait_ge(x_high, k + 1)
                sub(xl[:, k, :], y[:, k, :], xh[:, k, :]).then_inc(x_low, 1)
                if k < 2:
                    split_low(k, k, wh[k], wl[k])
            variance(1, rb, dense_ps(1))
            for i in range(HIST):
                last = dve.memset(inv_n[:, i:i + 1], 1.0 / (i + 1))
            last.then_inc(u_run, 1)
            dve.wait_ge(x_low, KT)
            dve.wait_ge(x_sq, KT)
            dve.memset(u_ext[:, 0:HIST], 0.0).then_inc(u_run, 1)
            inverse(1, rb)
            runs = 2
            dve.wait_ge(state_in, 16)

            S0 = HIST + SEQ
            for g, w in enumerate(POOL_WINDOWS):
                dve.wait_ge(tile_mm, g + 1)
                src = ps[:, NB * (g % 2):NB * (g % 2) + NB, :]
                if g:
                    dve.wait_ge(u_out, 32 * g)
                    dve.wait_ge(u_diff, g)
                dve.tensor_tensor(u_ext[:, HIST:HIST + 2 * BW].rearrange("p (a b) -> p a b", a=2), src[:, 0:2, 0:BW],
                                  rb[:, 0:2 * BW].rearrange("p (a b) -> p a b", a=2), ALU.mult)
                dve.tensor_tensor(u_ext[:, HIST + 2 * BW:S0], src[:, 2, 0:BW - DEC], rb[:, 2 * BW:SEQ], ALU.mult)
                dve.tensor_tensor(u_ext[:, S0 + HIST:UCOLS], src[:, 2, BW - DEC:BW], rb[:, SEQ:TOK], ALU.mult)
                dve.tensor_copy(u_ext[:, S0:S0 + HIST], state[:, g, :]).then_inc(tile_out, 1)
                split_low(g + 2, g % 2, wh[g % 2], wl[g % 2])
                if g == GROUPS - 1:
                    split_low(W_U + 2, 0, wh3, wl3)
                dve.wait_ge(tile_out, g + 1)
                dve.wait_ge(u_run, runs)
                a, shift, i = u_ext, 1, 0
                while shift < w:
                    o = run_sum[i % 2]
                    dve.tensor_tensor(o[:, shift:UCOLS], a[:, shift:UCOLS], a[:, 0:UCOLS - shift], ALU.add)
                    dve.tensor_copy(o[:, 0:shift], a[:, 0:shift]).then_inc(u_run, 1)
                    runs += 1
                    dve.wait_ge(u_run, runs)
                    a, shift, i = o, 2 * shift, i + 1
                if g:
                    dve.wait_ge(pool_mm, g)
                for o0, c0, n in ((0, HIST, SEQ), (SEQ, S0 + HIST, DEC)):
                    last = dve.scalar_tensor_tensor(out=diff[:, o0:o0 + n], in0=a[:, c0:c0 + n], scalar=1.0 / w,
                                                    in1=u_ext[:, c0:c0 + n], op0=ALU.mult, op1=ALU.subtract)
                last.then_inc(u_run, 1)
                runs += 1
                dve.wait_ge(u_run, runs)
                dve.tensor_tensor(diff[:, 0:w - 1], a[:, HIST:HIST + w - 1], inv_n[:, 0:w - 1], ALU.mult)\
                    .then_inc(u_run, 1)
                runs += 1
                dve.wait_ge(u_run, runs)
                sub(diff[:, 0:w - 1], diff[:, 0:w - 1], u_ext[:, HIST:HIST + w - 1]).then_inc(u_diff, 1)

            def block_t(j, c):
                t, b = c % 3, c // 3
                tok, n = ABLK[b]
                dve.wait_ge(blk_mm, block_no(j, c))
                stores = k_out if t == K else v_out
                if t == Q and not (isinstance(j, int) and j == 0 and b == 0):
                    dve.wait_ge(q_dup, 6 * j + 2 * b)
                if t != Q:
                    if b == 2:
                        dve.wait_ge(stores, 32 * j + 16)
                    elif b == 0 and not (isinstance(j, int) and j == 0):
                        dve.wait_ge(stores, 32 * j)
                    dve.tensor_tensor(tb[:, t, 0:n], ps[:, c % 2, 0:n], rb[:, tok:tok + n], ALU.mult).then_inc(blk_t, 1)
                else:
                    dve.scalar_tensor_tensor(out=tb[:, t, 0:n], in0=ps[:, c % 2, 0:n], scalar=QSCALE,
                                             in1=rb[:, tok:tok + n], op0=ALU.mult, op1=ALU.mult).then_inc(blk_t, 1)

            def block_low(j, c):
                t, b = c % 3, c // 3
                tok, n = ABLK[b]
                dve.wait_ge(blk_t, block_no(j, c))
                if t == K:
                    for h in range(2):
                        r, o = slice(64 * h, 64 * h + 64), slice(64 - 64 * h, 128 - 64 * h)
                        dve.wait_ge(blk_high, high_no(j, c, h))
                        i = sub(kk[h][o, tok:tok + n], tb[r, K, 0:n], kk[h][r, tok:tok + n])
                    i.then_inc(blk_low, 1)
                else:
                    for h in range(2):
                        r = slice(64 * h, 64 * h + 64)
                        dve.wait_ge(blk_high, high_no(j, c, h))
                        i = sub(q_l[h][r, b % 2, 0:n], tb[r, Q, 0:n], q_h[h][r, b % 2, 0:n])
                    i.then_inc(blk_low, 1)

            def v_low(j, c):
                b = c // 3
                dve.wait_ge(blk_high, high_no(j, c, 0))
                if b < 2:
                    sub(v_l[:, 3 * b:3 * b + 3, :], ps[:, c % 2, 0:384].rearrange("p (t d) -> p t d", d=P),
                        v_h[:, 3 * b:3 * b + 3, :]).then_inc(blk_low, 1)
                else:
                    sub(v_l[:, 6:8, :], ps[:, c % 2, 0:256].rearrange("p (t d) -> p t d", d=P), v_h[:, 6:8, :])
                    sub(v_l[0:DEC, 8, :], ps[0:DEC, c % 2, 256:384], v_h[0:DEC, 8, :]).then_inc(blk_low, 1)

            def turned_low(j, u):
                cols = 256 if u < SAMPLE_UNIT else 64
                p = parts(n_tiles(u))
                for n, (i0, i1) in enumerate(p):
                    dve.wait_ge(t_high, turned_no(j, u) - (len(p) - 1 - n))
                    sub(pt_l[:, i0:i1, 0:cols], turned[:, i0:i1, 0:cols], pt_h[:, i0:i1, 0:cols]).then_inc(t_low, 1)

            def maxima(j, u):
                dve.wait_ge(s_mm, head_no(j, u, 0))
                if u == 0:
                    dve.wait_ge(bias_in, 16 * j + 16)
                if u == SAMPLE_UNIT:
                    dve.wait_ge(bias_s_in, 32 * j + 32)
                if not (isinstance(j, int) and j == 0 and u == 0):
                    dve.wait_ge(t_mm, turned_no(j, u - 1) if u > 0 else turned_no(j - 1, 8))
                apart(dve)
                if u < SAMPLE_UNIT:
                    lo = WIN - P * n_tiles(u)
                    for h in range(2):
                        if h == 1:
                            dve.wait_ge(s_mm, head_no(j, u, 1))
                            apart(dve)
                        c0 = score_cols(h)
                        dve.tensor_tensor_reduce(out=prob[:, h, lo:WIN], in0=flat[:, c0 + lo:c0 + WIN],
                                                 in1=bias[:, h, lo:WIN], scale=-1.0, scalar=3.0e38, op0=ALU.add,
                                                 op1=ALU.min, accum_out=neg_max[:, h:h + 1]).then_inc(s_max, 1)
                else:
                    dve.tensor_tensor_reduce(out=prob[0:64, 0, 0:SKEYS],
                                             in0=flat[0:64, SAMPLE_COL:SAMPLE_COL + SKEYS],
                                             in1=bias_s[0:64, :], scale=-1.0, scalar=3.0e38, op0=ALU.add,
                                             op1=ALU.min, accum_out=neg_max[0:64, 0:1]).then_inc(s_max, 1)

            def inverses(j, u):
                rows = P if u < SAMPLE_UNIT else 64
                dve.wait_ge(s_exp, head_no(j, u, 0))
                dve.reciprocal(inv_sum[0:rows, 0:1], row_sum[0:rows, 0:1]).then_inc(s_inv[0], 1)
                if u < SAMPLE_UNIT:
                    dve.wait_ge(s_exp, head_no(j, u, 1))
                    dve.reciprocal(inv_sum[:, 1:2], row_sum[:, 1:2]).then_inc(s_inv[1], 1)
                    dve.wait_ge(s_inv[1], second_no(j, u))
                    apart(dve)
                    pr = prob[:, 1, WIN - P * n_tiles(u):WIN]
                    dve.tensor_scalar(pr, pr, inv_sum[:, 1:2], 1.0, ALU.mult, ALU.mult).then_inc(s_norm[1], 1)

            def split_cache(j):
                dve.wait_ge(w_high, 4 * j + W_U + 4)
                raw = w_raw[1][:, :, :].rearrange("p k n -> p (k n)")
                for h in range(2):
                    r, o = slice(64 * h, 64 * h + 64), slice(64 - 64 * h, 128 - 64 * h)
                    sub(kc[h][o, :], raw[r, 0:CACHE], kc[h][r, :])
                sub(vc_l[:, :, :], raw[:, CACHE:2 * CACHE].rearrange("p (t d) -> p t d", d=P), vc_h[:, :, :])\
                    .then_inc(w_low, 1)

            def slot(j, c, unit, prev):
                if c is not None:
                    if c == 0 and not (isinstance(j, int) and j == 0):
                        block_t(j - 1, 8)
                        block_low(j - 1, 8)
                    if c > 0:
                        block_t(j, c - 1)
                        if (c - 1) % 3 == K:
                            block_low(j, c - 1)
                elif unit and unit[1] == 6:
                    block_t(j - 1, 8)
                    block_low(j - 1, 8)
                if prev:
                    turned_low(*prev)
                if c is not None and c % 3 == 2:
                    v_low(j, c - 1)
                if unit:
                    maxima(*unit)
                    inverses(*unit)
                if c is not None and (c - 1) % 3 == Q:
                    block_low(j, c - 1)
                if c is not None:
                    if c == 0 and not (isinstance(j, int) and j == 0):
                        split_low(4 * j + W_U + 2, 0, wh3, wl3)
                    if c == 3:
                        split_cache(j)
                    if c == 7:
                        split_low(4 * j + W_U + 4, 0, wh[0], wl[0])
                    if c == 8:
                        split_low(4 * j + W_U + 5, 1, wh[1], wl[1])

            attention(dve, slot)

            for k in range(KT):
                dve.wait_ge(mix_high, k + 1)
                sub(ml[:, k, :], mix[:, k, :], mh[:, k, :]).then_inc(mix_low, 1)

            with dve.Fori(0, KT // 2) as i:
                for s in range(2):
                    ahead(2 * i + (D_OUT + s), s)

            def new_x(stage, n, g):
                variance(n, ss, dense_ps(0))
                inverse(n, ss)
                for k in range(KT + 2):
                    if k < KT:
                        dve.scalar_tensor_tensor(out=y[:, k, :], in0=y[:, k, :], scalar=vec[:, g, k:k + 1],
                                                 in1=ss[:, :], op0=ALU.mult, op1=ALU.mult).then_inc(scaled, 1)
                    if k >= 2 and stage < 3:
                        dve.wait_ge(x_high, KT * stage + k - 1)
                        sub(xl[:, k - 2, :], y[:, k - 2, :], xh[:, k - 2, :]).then_inc(x_low, 1)

            new_x(1, 2, 0)
            variance(3, rb, dense_ps(1))
            inverse(3, rb)

            def hidden_step(d, s, n, m):
                dve.wait_ge(tile_mm, d + 1)
                if not (isinstance(n, int) and n == 0):
                    dve.wait_ge(hid_low, n)
                    dve.wait_ge(hid_high, n)
                dve.scalar_tensor_tensor(out=blocks(tmp[:, :]), in0=dense_ps(s), scalar=0.0, in1=blocks(rb[:, :]),
                                         op0=ALU.max, op1=ALU.mult).then_inc(tile_out, 1)
                ahead(d, s)
                dve.wait_ge(hid_high, n + 1)
                sub(ml[:, bass.ds(m, 1), :].rearrange("p a t -> p (a t)"), tmp[:, :],
                    mh[:, bass.ds(m, 1), :].rearrange("p a t -> p (a t)")).then_inc(hid_low, 1)

            def ff_chunk(c, peel=False):
                if peel:
                    hidden_step(2 * KT * c + D_FF, 0, KT * c, 0)
                    hidden_step(2 * KT * c + D_FF + 1, 1, KT * c + 1, 1)
                with dve.Fori(1 if peel else 0, KT // 2) as i:
                    for s in range(2):
                        hidden_step(2 * KT * c + 2 * i + (D_FF + s), s, KT * c + 2 * i + s, 2 * i + s)
                with dve.Fori(0, KT // 2) as i:
                    for s in range(2):
                        d = 2 * KT * c + 2 * i + (D_FF + KT + s)
                        ahead(d, s)
                        ym = blocks(y[:, bass.ds(2 * i + s, 1), :].rearrange("p a t -> p (a t)"))
                        if peel:
                            dve.tensor_copy(ym, dense_ps(s)).then_inc(tile_out, 1)
                        else:
                            dve.wait_ge(tile_out, d - KT)
                            dve.tensor_tensor(ym, ym, dense_ps(s), ALU.add).then_inc(tile_out, 1)

            ff_chunk(0, True)
            with dve.Fori(1, FF_CHUNKS) as c:
                ff_chunk(c)

            def wp_part(m, s):
                dve.wait_ge(wp_high, m + 1)
                sub(wp_l[s][:, :, :], wp_raw[:, bass.ds(m, 1), :, :].rearrange("p a k n -> p (a k) n"),
                    wp_h[s][:, :, :]).then_inc(wp_low, 1)

            new_x(2, 4, 1)
            dve.wait_ge(p_high, 1)
            sub(p_l[:, :, :], p_raw[:, :, :], p_h[:, :, :]).then_inc(p_low, 1)
            wp_part(0, 0)
            wp_part(1, 1)

            def gate_step(m, s, more):
                if more:
                    ahead(m + D_GATE, s)
                dve.wait_ge(gate_put, m + 1)
                dve.wait_ge(ple_mm, m + 1)
                dve.tensor_tensor(blocks(y[:, bass.ds(m, 1), :].rearrange("p a t -> p (a t)")), dense_ps(1),
                                  blocks(tmp[:, :]), ALU.mult).then_inc(gated, 1)
                if more:
                    wp_part(m + 2, s)

            with dve.Fori(0, KT // 2 - 1) as i:
                for s in range(2):
                    gate_step(2 * i + s, s, True)
            for s in range(2):
                gate_step(KT - 2 + s, s, False)
            new_x(3, 5, 2)

        @block.gpsimd
        def _(pool):
            pool.memset(ones[:, :], 1.0).then_inc(const_made, 1)
            pool.memset(ident[:, :], 0.0).then_inc(const_made, 1)
            pool.memset(neg[:, :], NEG).then_inc(const_made, 1)
            pool.wait_ge(const_made, 2)
            pool.affine_select(out=ident[:, :], in_=ident[:, :], compare_op=ALU.not_equal, fill=1.0, base=0,
                               pattern=[[-1, P]], channel_multiplier=1).then_inc(const_made, 1)
            pool.memset(q_s[:, :, :, :].bitcast(F32), 0.0).then_inc(qs_zero, 1)
            pool.wait_ge(gains_in, 16)

            def gain_tile(arrived, s, row):
                pool.wait_ge(raw_in[s], 16 * arrived)
                apart(pool)
                g = gain[:, bass.ds(row, 1), :].rearrange("p a k -> p (a k)").unsqueeze(2).to_broadcast([P, KT, P])
                pool.tensor_tensor(w_raw[s][:, :, :], w_raw[s][:, :, :], g, ALU.mult).then_inc(w_gained, 1)

            for w in range(W_U + 3):
                gain_tile(w // 2 + 1, w % 2, 0)

            def scale_rows(j, u):
                whole = u < SAMPLE_UNIT
                pool.wait_ge(s_inv[0], unit_no(j, u))
                apart(pool)
                lo = WIN - P * n_tiles(u)
                pr = prob[:, 0, lo:WIN] if whole else prob[0:64, 0, 0:SKEYS]
                iv = inv_sum[:, 0:1] if whole else inv_sum[0:64, 0:1]
                pool.tensor_scalar(pr, pr, iv, 1.0, ALU.mult, ALU.mult).then_inc(s_norm[0], 1)

            def queries_low(j, c, unit):
                b, n = c // 3, ABLK[c // 3][1]
                if unit:
                    pool.wait_ge(s_norm[0], unit_no(*unit))
                pool.wait_ge(blk_high, high_no(j, c, 3))
                apart(pool)
                for h in range(2):
                    r, o = slice(64 * h, 64 * h + 64), slice(64 - 64 * h, 128 - 64 * h)
                    pool.tensor_tensor(q_l[h][o, b % 2, 0:n], tb[r, Q, 0:n], q_h[h][r, b % 2, 0:n], ALU.subtract)\
                        .then_inc(q_dup, 1)
                    pool.wait_ge(q_dup, 6 * j + 2 * b + h + 1)
                apart(pool)

            def place_queries(j):
                pool.wait_ge(blk_low, block_no(j, 6 + Q))
                pool.wait_ge(blk_high, high_no(j, 6 + Q, 3))
                pool.wait_ge(q_dup, 6 * j + 6)
                if isinstance(j, int) and j == 0:
                    pool.wait_ge(qs_zero, 1)
                else:
                    pool.wait_ge(s_mm, head_no(j - 1, 8, 0))
                apart(pool)
                for part, q in enumerate((q_h, q_l)):
                    for h in range(2):
                        pool.tensor_copy(q_s[:, part, h, DEC * h:DEC * h + DEC], q[h][:, 0, 256:256 + DEC])\
                            .then_inc(qs_put, 1)

            def slot(j, c, unit, prev):
                if unit:
                    if unit[1] == 6:
                        place_queries(unit[0])
                    scale_rows(*unit)
                if c is not None and c % 3 == 1:
                    queries_low(j, c - 1, unit)
                if c is not None and c >= 6:
                    gain_tile(2 * j + (5, 5, 6)[c - 6], (0, 1, 0)[c - 6], j + 1)

            attention(pool, slot)

            def sum_squares(n):
                pool.wait_ge(sq_sum, n + 1)
                pool.tensor_tensor(ss[:, :], ss[:, :], tmp[:, :], ALU.add).then_inc(sq_sum, 1)

            def sum_parts(out, m, n):
                o = out[:, bass.ds(m, 1), :].rearrange("p a t -> p (a t)")
                pool.tensor_tensor(o, xh[:, bass.ds(m, 1), :].rearrange("p a t -> p (a t)"),
                                   xl[:, bass.ds(m, 1), :].rearrange("p a t -> p (a t)"), ALU.add).then_inc(xsum_put, 1)

            pool.wait_ge(blk_mm, BLOCKS * PAIRS)
            pool.memset(ss[:, :], 0.0).then_inc(sq_sum, 1)

            def dense_gain(i, s):
                gain_tile(i + (D_OUT + R_OF_D) // 2 + 2 + s, 1 - s, i + PAIRS + 1 + s)

            with pool.Fori(0, KT // 2) as i:
                for s in range(2):
                    dense_gain(i, s)
                    m = 2 * i + s
                    sum_parts(xsum, m, m)
                    pool.wait_ge(tile_out, m + D_OUT + 1)
                    sum_squares(m)

            def new_x(stage, parts):
                pool.wait_ge(xsum_put, KT * stage)
                for k in range(KT):
                    pool.wait_ge(scaled, KT * (stage - 1) + k + 1)
                    pool.tensor_tensor(y[:, k, :], y[:, k, :], parts[:, k, :], ALU.add).then_inc(added, 1)

            new_x(1, xsum)
            pool.memset(ss[:, :], 0.0).then_inc(zeroed, 1)
            with pool.Fori(KT // 2, (D_GATE - D_OUT - KT) // 2) as i:
                for s in range(2):
                    dense_gain(i, s)
            pool.wait_ge(tile_mm, D_GATE - KT)
            pool.wait_ge(zeroed, 1)
            with pool.Fori((D_GATE - D_OUT - KT) // 2, (D_GATE - D_OUT) // 2) as i:
                for s in range(2):
                    dense_gain(i, s)
                    m = 2 * i + (s - (D_GATE - D_OUT - KT))
                    sum_parts(xsum, m, m)
                    pool.wait_ge(sq_put, m + 1)
                    sum_squares(m + KT)
            new_x(2, xsum)
            pool.memset(ss[:, :], 0.0).then_inc(zeroed, 1)
            pool.wait_ge(zeroed, 2)
            pool.wait_ge(p_low, 1)
            for m in range(KT):
                if m < KT - 3:
                    dense_gain((D_GATE - D_OUT + m) // 2, m % 2)
                if m == 0:
                    pool.wait_ge(x_low, 3 * KT)
                sum_parts(xsum2, m, m)
                pool.wait_ge(sq_put, KT + m + 1)
                sum_squares(2 * KT + m)
            new_x(3, xsum2)


def kernel(**inputs):
    import numpy as np
    import concourse.bacc as bacc
    from concourse.bass_utils import run_bass_kernel_spmd

    a = {k: np.asarray(v) for k, v in inputs.items()}
    one = np.float32(1)

    def feature_major(prompt, sample):
        return np.concatenate([prompt, sample], 0).T.reshape(-1, P, TOK)

    def tiles(w):
        k, m = w.shape
        return w.reshape(k // P, P, m // P, P).transpose(2, 1, 0, 3).reshape(m // P, P, -1)

    w_in = tiles(a["w_in"][0])
    q, k, v, u = (w_in[4 * i:4 * i + 4] for i in range(4))
    cache_k = a["cache_k"][0, 0].transpose(1, 2, 0).reshape(PAIRS, P, CACHE)
    cache_v = a["cache_v"][0, 0].reshape(4, P, PAIRS, P).transpose(2, 1, 0, 3).reshape(PAIRS, P, CACHE)
    cache = np.concatenate([cache_k, cache_v], 2)
    stream = [u] + [t[j:j + 1] for j in range(PAIRS) for t in (q, v, k, cache)] + [tiles(a["w_out"][0])]
    ff1, ff2 = tiles(a["w_ff1"][0]), a["w_ff2"][0]
    for c in range(FF_CHUNKS):
        stream += [ff1[KT * c:KT * c + KT], tiles(ff2[D_MODEL * c:D_MODEL * c + D_MODEL])]
    stream.append(tiles(a["w_ple_gate"][0]))
    w_stream = np.concatenate(stream, 0)

    def columns(g):
        return g.reshape(-1, P).T

    none = np.full((P, KT), one)
    rows = [columns(a["g_mix_pre"][0])] * PAIRS + [none] * 4
    rows += ([columns(a["g_ff_pre"][0])] * 4 + [none] * 4) * FF_CHUNKS + [none] * 4
    gains = np.stack(rows, 1)
    scale = np.concatenate([columns(a["pool_scale"][0]), np.zeros((P, KT - GROUPS), np.float32)], 1)
    vecs = np.stack([columns(a[g][0]) for g in ("g_mix_post", "g_ff_post", "g_ple_post")] + [scale], 1)
    rel = a["rel_bias"][0]
    bias_ext = np.concatenate([np.repeat(rel[:, 256:257], LEFT - 1, 1), rel[:, 256:0:-1]], 1)
    arrays = {
        "x_t": feature_major(a["x_prompt"][0], a["x_sample"][0]),
        "p_t": feature_major(a["p_prompt"][0, 0], a["p_sample"][0, 0]).transpose(1, 0, 2),
        "w_stream": w_stream,
        "w_ple": tiles(a["w_ple"][0]).reshape(KT, P, 2, P).transpose(1, 0, 2, 3),
        "gains": gains,
        "vecs": vecs,
        "w_pool": a["w_pool"][0].transpose(1, 0, 2),
        "state_t": a["state_pool"][0, 0].T.reshape(GROUPS, P, HIST).transpose(1, 0, 2),
        "bias_ext": bias_ext,
    }
    arrays = {n: np.ascontiguousarray(x) for n, x in arrays.items()}
    outs = {"y_t": (KT, P, TOK), "k_new": (PAIRS, P, CACHE + DEC), "v_new": (PAIRS, P, CACHE + DEC),
            "pool_p": (GROUPS, P, HIST), "pool_s": (GROUPS, P, HIST)}
    nc = bacc.Bacc("TRN2", target_bir_lowering=False, num_devices=1)
    args = {n: nc.dram_tensor(n, x.shape, mybir.dt.from_np(x.dtype), kind="ExternalInput").ap()
            for n, x in arrays.items()}
    args |= {n: nc.dram_tensor(n, s, F32, kind="ExternalOutput").ap() for n, s in outs.items()}
    build(nc, **args)
    got = run_bass_kernel_spmd(nc, [arrays], core_ids=[0]).results[0]
    y = got["y_t"].reshape(D_MODEL, TOK).T
    k, v = (got[n].reshape(N_HEADS, HEAD, CACHE + DEC).transpose(2, 0, 1) for n in ("k_new", "v_new"))
    pp, pq = (got[n].reshape(GROUPS * P, HIST).T for n in ("pool_p", "pool_s"))
    return (y[None, :SEQ], y[None, SEQ:], k[None, None, :CACHE], v[None, None, :CACHE], pp[None, None],
            k[None, None, CACHE:], v[None, None, CACHE:], pq[None, None])
```

```python
from contextlib import ExitStack

import concourse.bass as bass
from concourse import mybir

F32 = mybir.dt.float32
F32R = mybir.dt.float32r
ALU = mybir.AluOpType
ACT = mybir.ActivationFunctionType

P = 128
D_MODEL = 1024
KT = D_MODEL // P
SEQ, DEC = 1024, 32
TOK = SEQ + DEC
NB, BW = 3, TOK // 3
CHUNK, LEFT = 64, 512
N_HEADS, HEAD = 8, 64
PAIRS = N_HEADS // 2
WIN = LEFT + 2 * CHUNK
CACHE = 512
SKEYS = CACHE + DEC
EXT = WIN + P - 1
POOL_WINDOWS = (2, 4, 8, 16)
GROUPS = len(POOL_WINDOWS)
HIST = max(POOL_WINDOWS) - 1
UCOLS = HIST + SEQ + HIST + DEC
FF_CHUNKS = 4
EPS = 1e-6
NEG = -1e30
QSCALE = HEAD ** -0.5

ABLK = ((0, 384), (384, 384), (768, 288))
SAMPLE_UNIT = SEQ // P
UNITS = SAMPLE_UNIT + 1
BLOCKS = 9
Q, V, K = 0, 1, 2

MIX_ORDER = (0, 1, 2, 4, 3, 5, 6, 7)
MAP_BANKS = (3, 0, 5, 5)
DVE_ADDS = (1, 3, 6)

W_U = GROUPS
D_OUT = 4
D_FF = D_OUT + KT
D_GATE = D_FF + 2 * KT * FF_CHUNKS
D_END = D_GATE + KT
W_OF_D = 3 * PAIRS
R_OF_D = 4 * PAIRS
N_RAW = D_END + R_OF_D
GAIN_ROWS = PAIRS + (D_END - D_OUT) // 2


def n_tiles(u):
    return min(u + 1, 5) if u < SAMPLE_UNIT else 5


def unit_no(j, u):
    return UNITS * j + u + 1


def head_no(j, u, h):
    return (2 * UNITS - 1) * j + 2 * u + h + 1


def x_no(stage, b, k):
    return KT * (NB * stage + b) + k + 1


def norm_no(i, b):
    return NB * i + b + 1


def pair_no(i, b, s):
    return 2 * (NB * i + b) + s + 1


def sum_no(i, m):
    return (KT - 1) * i + m + 1


def turned_no(j, u):
    return 15 * j + (u + 1 if u < 3 else 3 + 2 * (u - 2))


def second_no(j, u):
    return SAMPLE_UNIT * j + min(u, SAMPLE_UNIT - 1) + 1


def block_no(j, c):
    return BLOCKS * j + c + 1


HIGH_COPIES = (4, 1, 2)


def high_no(j, c, n):
    return 21 * j + 7 * (c // 3) + sum(HIGH_COPIES[:c % 3]) + n + 1


def build(nc, x_t, p_t, w_stream, w_ple, gains, vecs, w_pool, state_t, bias_ext,
          y_t, k_new, v_new, pool_p, pool_s):
    bias_rows = nc.dram_tensor("bias_rows", (N_HEADS, P, WIN), F32, kind="Internal").ap()

    TILE = TOK * 4
    ACTS = KT * TILE
    base = 16512

    def at(name, shape, off, dt=F32):
        return nc.alloc_sbuf_tensor_at(name, [P] + shape, dt, offset=base + off)

    o_xh, o_xl, o_mh, o_ml, o_y = (i * ACTS for i in range(5))
    o_w = 5 * ACTS
    o_rb = o_w + 6 * 4096
    o_ss = o_rb + TILE
    o_tb = o_ss + TILE
    o_const = o_tb + 4 * 1536

    xh = at("xh", [KT, TOK], o_xh, F32R)
    xl = at("xl", [KT, TOK], o_xl, F32R)
    xsum = at("xsum", [KT, TOK], o_xl)
    mh = at("mh", [KT, TOK], o_mh, F32R)
    ml = at("ml", [KT, TOK], o_ml, F32R)
    mix = at("mix", [KT, TOK], o_ml)
    xsq = at("xsq", [KT, TOK], o_ml)
    y = at("y", [KT, TOK], o_y)

    w_raw = [at(f"w_raw{s}", [KT, P], o_w + s * 4096) for s in range(2)]
    wh = [at(f"wh{s}", [KT, P], o_w + (2 + s) * 4096, F32R) for s in range(2)]
    wl = [at(f"wl{s}", [KT, P], o_w + (4 + s) * 4096, F32R) for s in range(2)]
    rb = at("rb", [TOK], o_rb)
    ss = at("ss", [TOK], o_ss)
    tb = at("tb", [4, 384], o_tb)
    tmp = at("tmp", [TOK], o_tb)
    sig_b = [at(f"sig_b{s}", [BW], o_tb + s * BW * 4) for s in range(2)]
    sq_b = [at(f"sq_b{s}", [BW], o_tb + (2 + s) * BW * 4) for s in range(2)]
    pool_w = at("pool_w", [GROUPS, P], o_mh + 22272)

    ones = at("ones", [P], o_const)
    ident = at("ident", [P], o_const + 512)
    gain = at("gain", [GAIN_ROWS, KT], o_const + 1024)
    vec = at("vec", [4, KT], o_const + 2432)
    state = at("state", [GROUPS, HIST], o_const + 2560)
    inv_n = at("inv_n", [16], o_const + 2816)
    neg_max = at("neg_max", [2], o_const + 2880)
    row_sum = at("row_sum", [2], o_const + 2912)
    inv_sum = at("inv_sum", [2], o_const + 2944)
    eps = at("eps", [1], o_const + 2976)
    warmed = at("warmed", [1], o_const + 3008)

    q_h = [at(f"q_h{h}", [2, 384], o_mh + h * 3072, F32R) for h in range(2)]
    q_l = [at(f"q_l{h}", [2, 384], o_mh + (2 + h) * 3072, F32R) for h in range(2)]
    kk = [at(f"kk{h}", [TOK], o_mh + 12288 + h * TILE, F32R) for h in range(2)]
    v_h = at("v_h", [9, P], o_mh + 20736, F32R)
    v_l = at("v_l", [9, P], o_mh + 25344, F32R)
    q_s = at("q_s", [2, 2, 64], o_mh + 29952, F32R)
    bias_s = at("bias_s", [SKEYS], o_mh + 30976)
    pt_h = at("pt_h", [5, 256], o_y, F32R)
    pt_l = at("pt_l", [5, 256], o_y + 5120, F32R)
    prob = at("prob", [2, WIN], o_y + 10240)
    vc_h = at("vc_h", [4, P], o_y + 15360, F32R)
    vc_l = at("vc_l", [4, P], o_y + 17408, F32R)
    bias = at("bias", [2, WIN], o_y + 19456)
    kc = [at(f"kc{h}", [CACHE], o_y + 24576 + h * 2048, F32R) for h in range(2)]
    wh3 = at("wh3", [KT, P], o_ss, F32R)
    wl3 = at("wl3", [KT, P], o_y + 28672, F32R)
    a_wh, a_wl = (wh[0], wh[1], wh3), (wl[0], wl[1], wl3)
    neg = at("neg", [CHUNK], o_mh)
    u_exts = [at(f"u_ext{i}", [UCOLS], o_y + o) for i, o in enumerate((0, 17280, 21632))]
    run_sum = [at("run_sum0", [UCOLS], o_y + 4352), at("run_sum1", [UCOLS], o_y + 8704)]
    diff = at("diff", [TOK], o_y + 13056)
    p_h = at("p_h", [2, TOK], o_mh, F32R)
    p_l = at("p_l", [2, TOK], o_mh + 2 * TILE, F32R)
    wp_h = [at(f"wp_h{s}", [2, P], o_mh + 4 * TILE + s * 1024, F32R) for s in range(2)]
    wp_l = [at(f"wp_l{s}", [2, P], o_mh + 4 * TILE + 2048 + s * 1024, F32R) for s in range(2)]
    wp_raw = at("wp_raw", [KT, 2, P], o_mh + 4 * TILE + 4096)
    p_raw = at("p_raw", [2, TOK], o_ml)
    xsum2 = at("xsum2", [KT, TOK], o_ml)

    with ExitStack() as ctx:
        ps = ctx.enter_context(nc.psum_tensor("ps", [P, 8, 512], F32))
        flat = ps[:, :, :].rearrange("p a b -> p (a b)")

        def dense_ps(s):
            return ps[:, NB * s:NB * s + NB, 0:BW]

        def cols(b):
            return slice(b * BW, (b + 1) * BW)

        def blocks(t):
            return t.rearrange("p (a b) -> p a b", a=NB)

        def score_cols(h):
            return 2 * 512 + (128 if h == 0 else 768)

        SAMPLE_COL = 2 * 512
        pv_ps = flat[:, 5 * 512:5 * 512 + 256]
        turned = flat[:, 5 * 512 + 256:8 * 512].rearrange("p (t c) -> p t c", c=256)

        def parts(n):
            return ((0, min(n, 3)),) if n <= 3 else ((0, 3), (3, n))

        def sem(name):
            return ctx.enter_context(nc.semaphore(name))

        x_in = [[sem(f"x_in{b}_{q}") for q in range(4 if b == 0 else 2)] for b in range(NB)]
        raw_in = [sem("raw_in0"), sem("raw_in1")]
        vecs_in, pool_w_in, state_in, gains_in = sem("vecs_in"), sem("pool_w_in"), sem("state_in"), sem("gains_in")
        rows_in, corners_in, bias_in, bias_s_in = sem("rows_in"), sem("corners_in"), sem("bias_in"), sem("bias_s_in")
        p_in, wp_in = sem("p_in"), sem("wp_in")
        k_out, v_out, y_out = sem("k_out"), sem("v_out"), sem("y_out")
        u_out = [sem(f"u_out{g}") for g in range(GROUPS)]
        const_made = sem("const_made")
        w_gained, w_high, w_low = sem("w_gained"), sem("w_high"), sem("w_low")
        x_high, x_low, x_sq = sem("x_high"), sem("x_low"), sem("x_sq")
        x_even, x_odd, x_sums = sem("x_even"), sem("x_odd"), sem("x_sums")
        in_norm = [sem(f"in_{x}") for x in ("mm", "root", "inv")]
        out_norm = [sem(f"out_{x}") for x in ("mm", "root", "inv")]
        warm = sem("warm")
        pair_mm, y_blk, sq_blk, sum_blk, gate_blk = sem("pair_mm"), sem("y_blk"), sem("sq_blk"), sem("sum_blk"), sem("gate_blk")
        tile_mm, tile_out = sem("tile_mm"), sem("tile_out")
        u_run, u_diff, pool_mm, pool_put = sem("u_run"), sem("u_diff"), sem("pool_mm"), sem("pool_put")
        blk_mm, blk_t, blk_high, blk_low, v_turn = sem("blk_mm"), sem("blk_t"), sem("blk_high"), sem("blk_low"), sem("v_turn")
        q_dup = sem("q_dup")
        qs_zero, qs_put = sem("qs_zero"), sem("qs_put")
        s_mm, s_max, s_exp = sem("s_mm"), sem("s_max"), sem("s_exp")
        s_inv = [sem("s_inv0"), sem("s_inv1")]
        s_norm = [sem("s_norm0"), sem("s_norm1")]
        t_mm, t_high, t_low, pv_mm, mix_put = sem("t_mm"), sem("t_high"), sem("t_low"), sem("pv_mm"), sem("mix_put")
        mix_high, mix_low = sem("mix_high"), sem("mix_low")
        sq_put, sq_sum = sem("sq_put"), sem("sq_sum")
        scaled, added, added2, xsum_put = sem("scaled"), sem("added"), sem("added2"), sem("xsum_put")
        sq_done, hid_high, hid_low = sem("sq_done"), sem("hid_high"), sem("hid_low")
        p_high, p_low, wp_high, wp_low = sem("p_high"), sem("p_low"), sem("wp_high"), sem("wp_low")
        ple_mm, gate_put, gated, carried = sem("ple_mm"), sem("gate_put"), sem("gated"), sem("carried")

        block = ctx.enter_context(nc.Block())

        def apart(eng):
            eng.sem_inc(carried, 1)

        def wait_pair(eng, i, b, s):
            if b < NB - 1:
                eng.wait_ge(pair_mm, 4 * i + 2 * b + s + 1)
            else:
                eng.wait_ge(tile_mm, (D_FF, D_GATE, D_END)[i] - 1 + s)

        SLOT_UNITS = [(-1, 6), (-1, 7), (-1, 8), (0, 0), (0, 1), (0, 2), (0, 3), (0, 4), (0, 5)]

        def new_pair(j, c, unit):
            return c == 0 and not (isinstance(j, int) and j == 0) or c is None and bool(unit) and unit[1] == 6

        def attention(eng, slot):
            def run(j, first):
                for c in range(BLOCKS):
                    dj, u = SLOT_UNITS[c]
                    unit = None if first and dj < 0 else (j + dj, u)
                    up = (u - 1) % UNITS
                    prev = None if first and c <= 3 else (j + dj - (1 if u == 0 else 0), up)
                    slot(j, c, unit, prev)
            run(0, True)
            with eng.Fori(1, PAIRS) as j:
                run(j, False)
            last = PAIRS - 1
            slot(PAIRS, None, (last, 6), (last, 5))
            slot(PAIRS, None, (last, 7), (last, 6))
            slot(PAIRS, None, (last, 8), (last, 7))
            slot(PAIRS, None, None, (last, 8))

        @block.sync
        def _(sp):
            def load_raw(r, s):
                sp.dma_start(w_raw[s][:, :, :], w_stream[bass.ds(r, 1)].rearrange("a p (k n) -> p (a k) n", k=KT))\
                  .then_inc(raw_in[s], 16)

            def next_raw(r, s):
                sp.wait_ge(w_low, r - 1)
                load_raw(r, s)

            def load_bias(j):
                sp.dma_start(bias[:, :, :], bias_rows[bass.ds(2 * j, 2)].rearrange("h p c -> p h c"))\
                  .then_inc(bias_in, 16)

            def load_bias_s(j):
                for h in range(2):
                    sp.dma_start(bias_s[DEC * h:DEC * h + DEC, :],
                                 bias_rows[bass.ds(2 * j + h, 1), 0:DEC, 0:SKEYS].rearrange("a p c -> (a p) c"))\
                      .then_inc(bias_s_in, 16)

            load_raw(0, 0)
            for b in range(NB):
                n = KT // len(x_in[b])
                for q, arrived in enumerate(x_in[b]):
                    sp.dma_start(y[:, n * q:n * q + n, cols(b)], x_t[n * q:n * q + n, :, cols(b)].rearrange("k p t -> p k t"))\
                      .then_inc(arrived, 16)
                    if b == 0 and q == 0:
                        load_raw(1, 1)
            next_raw(2, 0)
            next_raw(3, 1)
            src = bass.AP(bias_ext.tensor, P - 1, [[EXT, N_HEADS], [-1, P], [1, WIN]])
            sp.dma_start(bias_rows, src).then_inc(rows_in, 16)
            sp.wait_ge(rows_in, 16)
            sp.wait_ge(const_made, 4)
            rows = bias_rows.rearrange("h p c -> p h c")
            for h in range(N_HEADS):
                sp.dma_start(rows[0:CHUNK, h, WIN - CHUNK:WIN], neg[0:CHUNK, :]).then_inc(corners_in, 16)
                sp.dma_start(rows[CHUNK:P, h, 0:CHUNK], neg[CHUNK:P, :]).then_inc(corners_in, 16)
            sp.wait_ge(corners_in, 16 * 2 * N_HEADS)
            for i in range(4):
                next_raw(W_U + i, i % 2)
            sp.wait_ge(x_low, NB * KT)
            sp.wait_ge(x_even, NB * KT // 2)
            sp.wait_ge(x_odd, NB * KT // 2)
            sp.wait_ge(u_diff, GROUPS - 1)
            sp.wait_ge(u_out[1], 32)
            sp.wait_ge(u_out[2], 32)
            load_bias(0)
            load_bias_s(0)
            with sp.Fori(1, PAIRS) as j:
                for i in range(4):
                    next_raw(4 * j + W_U + i, i % 2)
                sp.wait_ge(s_max, head_no(j - 1, 7, 1))
                load_bias(j)
                sp.wait_ge(s_max, head_no(j - 1, 8, 0))
                load_bias_s(j)
            with sp.Fori(0, (N_RAW - 4 * PAIRS - W_U) // 2) as i:
                for s in range(2):
                    next_raw(2 * i + (4 * PAIRS + W_U + s), s)
            for b in range(NB):
                for q in range(KT // 2):
                    by_dve = len([k for k in DVE_ADDS if k < 2 * q + 2])
                    sp.wait_ge(added, 2 * NB * KT + b * (KT - len(DVE_ADDS)) + 2 * q + 2 - by_dve)
                    sp.wait_ge(added2, b * len(DVE_ADDS) + by_dve)
                    sp.dma_start(y_t[2 * q:2 * q + 2, :, cols(b)].rearrange("k p t -> p k t"), y[:, 2 * q:2 * q + 2, cols(b)])\
                      .then_inc(y_out, 16)
            sp.wait_ge(y_out, 16 * NB * KT // 2)
            for g in range(GROUPS):
                sp.wait_ge(u_out[g], 32)
            sp.wait_ge(k_out, 16 * 2 * PAIRS)
            sp.wait_ge(v_out, 16 * 2 * PAIRS)

        @block.tensor
        def _(pe):
            def split3(out, w_hi, w_lo, a_hi, a_lo, first, last):
                pe.matmul(out, w_hi, a_hi, start=first, stop=False)
                pe.matmul(out, w_hi, a_lo, start=False, stop=False)
                return pe.matmul(out, w_lo, a_hi, start=False, stop=last)

            def dense_k(s, k, a_hi, a_lo):
                for b in range(NB):
                    mm = split3(ps[:, NB * s + b, 0:BW], wh[s][:, k, :], wl[s][:, k, :],
                                a_hi[:, k, b * BW:(b + 1) * BW], a_lo[:, k, b * BW:(b + 1) * BW],
                                k == 0, k == KT - 1)
                return mm

            def weights_ready(r):
                pe.wait_ge(w_high, r + 1)
                pe.wait_ge(w_low, r + 1)

            def dense_tile(d, s, a_hi, a_lo):
                weights_ready(d + R_OF_D)
                pe.wait_ge(tile_out, d - 1)
                for k in range(KT):
                    mm = dense_k(s, k, a_hi, a_lo)
                mm.then_inc(tile_mm, 1)

            def block_k(s, b, k, a_hi, a_lo):
                return split3(ps[:, NB * s + b, 0:BW], wh[s][:, k, :], wl[s][:, k, :],
                              a_hi[:, k, cols(b)], a_lo[:, k, cols(b)], k == 0, k == KT - 1)

            def out_sums(i, b):
                pe.wait_ge(sum_blk, pair_no(i, b, 1))
                if i < 2 and (i or b):
                    pe.wait_ge(out_norm[1], norm_no(i, b) - 1)
                if i == 2:
                    pe.wait_ge(gate_blk, pair_no(0, b, 0))
                pe.matmul(ps[:, b if i == 2 else 6, 0:BW], ones[:, :], ss[:, cols(b)], start=True, stop=True)\
                  .then_inc(out_norm[0], 1)

            def last_pair(i, d, a_hi, a_lo):
                for b in range(NB):
                    for s in range(2):
                        if b == 0:
                            weights_ready(d + s + R_OF_D)
                            pe.wait_ge(tile_out, d + s - 1)
                        for k in range(KT):
                            mm = block_k(s, b, k, a_hi, a_lo)
                        mm.then_inc(pair_mm if b < NB - 1 else tile_mm, 1)
                        if b and not s:
                            out_sums(i, b - 1)

            def square_sums(stage, i_in, b, k):
                pe.wait_ge(x_sq, x_no(stage - 1, b, k))
                if k == 0 and b:
                    pe.wait_ge(in_norm[1], norm_no(i_in, b - 1))
                mm = pe.matmul(ps[:, 7, 0:BW], ones[:, :], xsq[:, k, cols(b)], start=(k == 0), stop=(k == KT - 1))
                if k == KT - 1:
                    mm.then_inc(in_norm[0], 1)

            def first_pair(r, d, stage, i_in, i_out):
                for b in range(NB):
                    for s in range(2):
                        if stage == 0 and b and s:
                            x_square_sums(b - 1)
                        if b == 0:
                            weights_ready(r + s)
                            if d:
                                pe.wait_ge(tile_out, d + s - 1)
                        if b == NB - 1 and s == 0 and i_in is not None:
                            for k in range(KT):
                                square_sums(stage, i_in, b, k)
                        for k in range(KT):
                            if s == 0:
                                pe.wait_ge(x_high, x_no(stage, b, k))
                                pe.wait_ge(x_low, x_no(stage, b, k))
                            if b < NB - 1 and s == 0 and i_in is not None:
                                square_sums(stage, i_in, b, k)
                            mm = block_k(s, b, k, xh, xl)
                            if i_out is not None and (b, s, k) == (0, 1, 0):
                                out_sums(i_out, NB - 1)
                            if stage == 0 and (b, s, k) == (NB - 1, 1, 3):
                                x_square_sums(b)
                        if b == NB - 1:
                            mm.then_inc(tile_mm, 1)

            pe.wait_ge(const_made, 4)

            def x_square_sums(b):
                pe.wait_ge(x_sums, (KT - 1) * (b + 1))
                if b:
                    pe.wait_ge(in_norm[1], norm_no(0, b - 1))
                pe.matmul(ps[:, 7, 0:BW], ones[:, :], xsq[:, 0, cols(b)], start=True, stop=True)\
                  .then_inc(in_norm[0], 1)
            first_pair(0, 0, 0, None, None)

            def u_tile(g):
                weights_ready(g)
                pe.wait_ge(tile_out, g - 1)
                if g == 3:
                    pe.wait_ge(pool_put, 1)
                for k in range(KT):
                    if k == KT - 2:
                        pool_tile(g - 2)
                    mm = dense_k(g % 2, k, xh, xl)
                mm.then_inc(tile_mm, 1)

            def pool_tile(g):
                if g == 0:
                    pe.wait_ge(pool_w_in, 16)
                pe.wait_ge(tile_out, (2, 3, 4, 4)[g])
                if g == 3:
                    pe.wait_ge(pool_put, 3)
                pe.wait_ge(u_diff, g + 1)
                for b in range(NB):
                    mm = pe.matmul(ps[:, MAP_BANKS[g] + b, 0:BW], pool_w[:, g, :], diff[:, cols(b)],
                                   start=True, stop=True)
                mm.then_inc(pool_mm, 1)

            u_tile(2)
            u_tile(3)

            def first_out(n0, n1):
                if n0 == 0:
                    weights_ready(D_OUT + R_OF_D)
                    pe.wait_ge(tile_out, D_OUT - 1)
                    pe.wait_ge(blk_low, block_no(PAIRS - 1, BLOCKS - 1))
                    pe.wait_ge(s_max, head_no(PAIRS - 1, 8, 0))
                for n in range(n0, n1):
                    pe.wait_ge(mix_high, n + 1)
                    pe.wait_ge(mix_low, n + 1)
                    k = MIX_ORDER[n]
                    for b in range(NB):
                        mm = split3(ps[:, b, 0:BW], wh[0][:, k, :], wl[0][:, k, :], mh[:, k, cols(b)], ml[:, k, cols(b)],
                                    n == 0, n == KT - 1)
                if n1 == KT:
                    mm.then_inc(tile_mm, 1)

            def proj(j, c, half):
                t, (tok, n) = c % 3, ABLK[c // 3]
                out = ps[:, c % 2, 0:n]
                if half == 0:
                    if c < 3:
                        weights_ready(4 * j + W_U + t)
                    if not isinstance(j, int) or j > 0 or c >= 2:
                        before = c - 2 if c else -1
                        if before % 3 == V:
                            pe.wait_ge(blk_low, block_no(j, before if c > 1 else -2))
                        else:
                            pe.wait_ge(blk_t, block_no(j, before if c > 1 else -1 - c))
                for k in range(4 * half, 4 * half + 4):
                    mm = split3(out, a_wh[t][:, k, :], a_wl[t][:, k, :], xh[:, k, tok:tok + n], xl[:, k, tok:tok + n],
                                k == 0, k == KT - 1)
                if half:
                    mm.then_inc(blk_mm, 1)

            def turn_v(j, c):
                tok, n = ABLK[c // 3]
                pe.wait_ge(blk_t, block_no(j, c))
                for i in range(0, n, P):
                    m = min(P, n - i)
                    mm = pe.transpose(ps[0:m, c % 2, i:i + P], tb[:, 1, i:i + m], ident[:, :])
                mm.then_inc(v_turn, 1)

            def scores(j, u):
                if u < SAMPLE_UNIT:
                    b, n = u // 3, n_tiles(u)
                    pe.wait_ge(blk_low, block_no(j, 3 * b + K))
                    pe.wait_ge(blk_high, high_no(j, 3 * b + K, 1))
                    pe.wait_ge(q_dup, 6 * j + 2 * b + 2)
                    if isinstance(j, int) and j == 0 and u == 0:
                        pe.wait_ge(pool_put, GROUPS)
                    else:
                        pe.wait_ge(s_max, head_no(j, u - 1, 1))
                    lo = WIN - P * n
                    q0 = P * u - ABLK[b][0]
                    cuts = ((0, max(lo, 384), WIN), (1, lo, 256), (0, lo, 384), (1, max(lo, 256), WIN))
                    for i, (h, a, e) in enumerate(cuts):
                        if e > a:
                            out = flat[:, score_cols(h) + a:score_cols(h) + e]
                            key0 = P * (u + 1) - WIN + a
                            keys = kk[h][:, key0:key0 + e - a]
                            pe.matmul(out, q_h[h][:, b % 2, q0:q0 + P], keys, start=True, stop=False)
                            mm = pe.matmul(out, q_l[h][:, b % 2, q0:q0 + P], keys, start=False, stop=True)
                        if i >= 2:
                            mm.then_inc(s_mm, 1)
                else:
                    pe.wait_ge(qs_put, 4 * j + 4)
                    pe.wait_ge(s_max, head_no(j, u - 1, 1))
                    pe.wait_ge(w_low, 4 * j + W_U + 4)
                    for a, e in ((0, CACHE), (CACHE, SKEYS)):
                        out = flat[0:64, SAMPLE_COL + a:SAMPLE_COL + e]
                        for i in range(4):
                            h = i // 2
                            keys = kc[h][:, :] if a < CACHE else kk[h][:, SEQ:TOK]
                            mm = pe.matmul(out, q_s[:, i % 2, h, :], keys, start=(i == 0), stop=(i == 3))
                    mm.then_inc(s_mm, 1)

            def turn(j, u):
                n = n_tiles(u)
                whole = u < SAMPLE_UNIT
                pe.wait_ge(s_norm[0], unit_no(j, u))
                if u > 0 or not isinstance(j, int) or j > 0:
                    pe.wait_ge(t_low, turned_no(j, u - 1) if u > 0 else turned_no(j - 1, 8))
                    pe.wait_ge(mix_put, unit_no(j, u - 1))
                if not whole:
                    apart(pe)
                for i0, i1 in parts(n):
                    if whole:
                        for h in range(2):
                            if h == 1 and i0 == 0:
                                pe.wait_ge(s_norm[1], second_no(j, u))
                            for i in range(i0, i1):
                                c0 = WIN - P * n + P * i
                                mm = pe.transpose(turned[:, i, P * h:P * h + P], prob[:, h, c0:c0 + P], ident[:, :])
                    else:
                        for i in range(i0, i1):
                            m = P if i < 4 else DEC
                            mm = pe.transpose(turned[0:m, i, 0:64], prob[0:64, 0, P * i:P * i + m], ident[0:64, 0:64])
                    mm.then_inc(t_mm, 1)

            def weigh_values(j, u):
                n = n_tiles(u)
                pe.wait_ge(t_low, turned_no(j, u) - (len(parts(n)) - 1))
                whole = u < SAMPLE_UNIT
                pe.wait_ge(blk_low, block_no(j, 3 * (u // 3 if whole else 2) + V))
                cols = 256
                for i in range(n):
                    rows = P
                    if i == 3:
                        pe.wait_ge(t_low, turned_no(j, u))
                    if whole:
                        t = u + 1 - n + i
                        vh, vl = v_h[:, t, :], v_l[:, t, :]
                    elif i < 4:
                        vh, vl = vc_h[:, i, :], vc_l[:, i, :]
                    else:
                        rows = DEC
                        vh, vl = v_h[0:DEC, 8, :], v_l[0:DEC, 8, :]
                    mm = split3(pv_ps[:, 0:cols], vh, vl, pt_h[0:rows, i, 0:cols], pt_l[0:rows, i, 0:cols],
                                i == 0, i == n - 1)
                mm.then_inc(pv_mm, 1)

            def slot(j, c, unit, prev):
                if c is not None:
                    if isinstance(j, int) and j == 0:
                        if c == 0:
                            pe.wait_ge(pool_put, 2)
                        if c in (1, 2):
                            pool_tile(c + 1)
                    proj(j, c, 0)
                if c is not None and c % 3 == 2:
                    turn_v(j, c - 1)
                if unit:
                    scores(*unit)
                if prev:
                    weigh_values(*prev)
                if c is not None:
                    proj(j, c, 1)
                if unit:
                    turn(*unit)
                if c is None and prev[1] >= SAMPLE_UNIT - 1:
                    first_out(2 * (prev[1] - SAMPLE_UNIT + 1), 2 * (prev[1] - SAMPLE_UNIT + 2))

            attention(pe, slot)

            first_out(4, KT)
            dense_tile(D_OUT + 1, 1, mh, ml)
            with pe.Fori(1, KT // 2 - 1) as i:
                for s in range(2):
                    dense_tile(2 * i + (D_OUT + s), s, mh, ml)
            last_pair(0, D_FF - 2, mh, ml)

            first_pair(D_FF + R_OF_D, D_FF, 1, 1, 0)
            with pe.Fori(1, KT // 2) as i:
                for s in range(2):
                    dense_tile(2 * i + (D_FF + s), s, xh, xl)

            def second(c, last=False):
                d = 2 * KT * c + (D_FF + KT)
                weights_ready(d + R_OF_D)
                pe.wait_ge(tile_out, d - 1)
                for k in range(KT):
                    if k >= KT - 2:
                        pe.wait_ge(hid_low, KT * c + k + 1)
                    mm = dense_k(0, k, mh, ml)
                mm.then_inc(tile_mm, 1)
                dense_tile(d + 1, 1, mh, ml)
                with pe.Fori(1, KT // 2 - (1 if last else 0)) as i:
                    for s in range(2):
                        dense_tile(2 * KT * c + 2 * i + (D_FF + KT + s), s, mh, ml)

            second(0)
            def chunk(c, last):
                with pe.Fori(0, KT // 2) as i:
                    for s in range(2):
                        dense_tile(2 * KT * c + 2 * i + (D_FF + s), s, xh, xl)
                second(c, last)

            with pe.Fori(1, FF_CHUNKS - 1) as c:
                chunk(c, False)
            chunk(FF_CHUNKS - 1, True)
            last_pair(1, D_GATE - 2, mh, ml)

            def embed(q, bank, m, s, b):
                if not isinstance(q, int) or q >= 2:
                    pe.wait_ge(gated, q - 1)
                if b == 0:
                    pe.wait_ge(wp_low, m + 1)
                for k in range(2):
                    mm = split3(ps[:, 6 + bank, 0:BW], wp_h[s][:, k, :], wp_l[s][:, k, :],
                                p_h[:, k, cols(b)], p_l[:, k, cols(b)], k == 0, k == 1)
                mm.then_inc(ple_mm, 1)

            def embed_block(m, s, b):
                embed(NB * m + b, (s + b) % 2, m, s, b)

            def gate_tile(m, s):
                weights_ready(m + (D_GATE + R_OF_D))
                pe.wait_ge(gate_put, m - 1)
                for k in range(KT):
                    mm = dense_k(s, k, xh, xl)
                    if k == KT // 2 - 1:
                        embed_block(m - 1, 1 - s, 1)
                        embed_block(m - 1, 1 - s, 2)
                mm.then_inc(tile_mm, 1)
                embed_block(m, s, 0)

            first_pair(D_GATE + R_OF_D, D_GATE, 2, None, 1)
            pe.wait_ge(p_low, 1)
            pe.wait_ge(out_norm[1], norm_no(1, NB - 1))
            embed_block(0, 0, 0)
            embed_block(0, 0, 1)
            embed_block(0, 0, 2)
            embed_block(1, 1, 0)
            with pe.Fori(1, KT // 2 - 1) as i:
                for s in range(2):
                    gate_tile(2 * i + s, s)
            for b in range(NB):
                for s in range(2):
                    if b == 0:
                        weights_ready(D_END - 2 + s + R_OF_D)
                        pe.wait_ge(gate_put, KT - 3 + s)
                    for k in range(KT):
                        mm = block_k(s, b, k, xh, xl)
                    mm.then_inc(pair_mm if b < NB - 1 else tile_mm, 1)
                    if b == 0 and s == 0:
                        embed_block(KT - 3, 1, 1)
                        embed_block(KT - 3, 1, 2)
                    embed(NB * (KT - 2) + 2 * b + s, s, KT - 2 + s, s, b)
                    if b and not s:
                        out_sums(2, b - 1)
            out_sums(2, NB - 1)

        @block.scalar
        def _(act):
            def act_copy(out, in_):
                return act.activation(out, in_, ACT.Copy)

            def split_high(w, r, s, hi):
                act.wait_ge(w_gained, w + 1)
                act_copy(hi[:, :, :], w_raw[s][:, :, :]).then_inc(w_high, 1)

            def ahead(d, s):
                act.wait_ge(tile_mm, d + 1)
                split_high(d + 2 + W_OF_D, d + 2 + R_OF_D, s, wh[s])

            act.dma_start(gain[:, :, :], gains).then_inc(gains_in, 16)
            act.dma_start(vec[:, :, :], vecs).then_inc(vecs_in, 16)
            act.dma_start(pool_w[:, :, :], w_pool).then_inc(pool_w_in, 16)
            act.dma_start(state[:, :, :], state_t).then_inc(state_in, 16)

            def x_parts(stage, b, k, squares):
                act_copy(xh[:, k, cols(b)], y[:, k, cols(b)]).then_inc(x_high, 1)
                if squares:
                    act.activation(xsq[:, k, cols(b)], y[:, k, cols(b)], ACT.Square)\
                       .then_inc(x_sq if stage else x_even, 1)

            def root(norm, i, b, t):
                act.wait_ge(norm[0], norm_no(i, b))
                bank = 7 if norm is in_norm else 6 if i < 2 else b
                act.activation(t[:, cols(b)], ps[:, bank, 0:BW], ACT.Sqrt, scale=1.0 / D_MODEL, bias=eps[:, 0:1])\
                   .then_inc(norm[1], 1)

            def load_root_table():
                act.activation(warmed[:, :], eps[:, :], ACT.Sqrt).then_inc(warm, 1)

            for b in range(NB):
                for k in range(KT):
                    n = KT // len(x_in[b])
                    if k % n == 0:
                        act.wait_ge(x_in[b][k // n], 16)
                    x_parts(0, b, k, k % 2 == 0)
                    if b == 0 and k in (0, 4):
                        split_high(k // 4, k // 4, k // 4, wh[k // 4])
                if b == 0:
                    act.wait_ge(const_made, 5)
                else:
                    root(in_norm, 0, b - 1, rb)
            def store_u(g):
                act.wait_ge(tile_out, g + 1)
                u_ext = u_exts[g % 3]
                act.dma_start(pool_p[g], u_ext[:, SEQ:SEQ + HIST]).then_inc(u_out[g], 16)
                act.dma_start(pool_s[g], u_ext[:, UCOLS - HIST:UCOLS]).then_inc(u_out[g], 16)

            def put_group(g):
                if g == 0:
                    act.wait_ge(vecs_in, 16)
                act.wait_ge(pool_mm, g + 1)
                act.activation(blocks(mix[:, GROUPS + g, :]), ps[:, MAP_BANKS[g]:MAP_BANKS[g] + NB, 0:BW],
                               ACT.Identity, scale=vec[:, 3, g:g + 1]).then_inc(pool_put, 1)

            for g in range(GROUPS):
                if g >= 2:
                    put_group(g - 2)
                act.wait_ge(tile_mm, g + 1)
                split_high(g + 2, g + 2, g % 2, wh[g % 2])
                if g == 0:
                    root(in_norm, 0, NB - 1, rb)
                if g >= 1:
                    store_u(g - 1)
            split_high(W_U + 2, W_U + 2, 0, wh3)
            store_u(3)

            def mix_parts(n0, n1):
                for k in MIX_ORDER[n0:n1]:
                    act_copy(mh[:, k, :], mix[:, k, :]).then_inc(mix_high, 1)

            def block_high(j, c):
                t, b = c % 3, c // 3
                tok, n = ABLK[b]
                if t == V:
                    return
                act.wait_ge(blk_t, block_no(j, c))
                if t == K:
                    for h in range(2):
                        r = slice(64 * h, 64 * h + 64)
                        act_copy(kk[h][r, tok:tok + n], tb[r, K, 0:n]).then_inc(blk_high, 1)
                else:
                    for dup in range(2):
                        for h in range(2):
                            r = slice(64 * h, 64 * h + 64)
                            o = r if dup == 0 else slice(64 - 64 * h, 128 - 64 * h)
                            act_copy(q_h[h][o, b % 2, 0:n], tb[r, Q, 0:n]).then_inc(blk_high, 1)

            def store_block(j, c):
                t, b = c % 3, c // 3
                if t == Q or b == 0:
                    return
                act.wait_ge(blk_t, block_no(j, c))
                n0, o0 = (P, 0) if b == 1 else (0, 2 * P)
                new, stored = (k_new, k_out) if t == K else (v_new, v_out)
                act.dma_start(new[bass.ds(j, 1), :, o0:o0 + ABLK[b][1] - n0].rearrange("a p c -> (a p) c"),
                              tb[:, t, n0:ABLK[b][1]]).then_inc(stored, 16)

            def v_high(j, c):
                b = c // 3
                act.wait_ge(v_turn, 3 * j + b + 1)
                if b < 2:
                    act_copy(v_h[:, 3 * b:3 * b + 3, :],
                             ps[:, c % 2, 0:384].rearrange("p (t d) -> p t d", d=P)).then_inc(blk_high, 1)
                else:
                    act_copy(v_h[:, 6:8, :], ps[:, c % 2, 0:256].rearrange("p (t d) -> p t d", d=P))
                    act_copy(v_h[0:DEC, 8, :], ps[0:DEC, c % 2, 256:384]).then_inc(blk_high, 1)

            def turned_high(j, u):
                cols = 256 if u < SAMPLE_UNIT else 64
                p = parts(n_tiles(u))
                for n, (i0, i1) in enumerate(p):
                    act.wait_ge(t_mm, turned_no(j, u) - (len(p) - 1 - n))
                    act_copy(pt_h[:, i0:i1, 0:cols], turned[:, i0:i1, 0:cols]).then_inc(t_high, 1)

            def exps(j, u):
                if u < SAMPLE_UNIT:
                    lo = WIN - P * n_tiles(u)
                    for h in range(2):
                        act.wait_ge(s_max, head_no(j, u, h))
                        act.activation(prob[:, h, lo:WIN], prob[:, h, lo:WIN], ACT.Exp, scale=-1.0,
                                       bias=neg_max[:, h:h + 1], accum_out=row_sum[:, h:h + 1]).then_inc(s_exp, 1)
                else:
                    act.wait_ge(s_max, head_no(j, u, 0))
                    act.activation(prob[0:64, 0, 0:SKEYS], prob[0:64, 0, 0:SKEYS], ACT.Exp, scale=-1.0,
                                   bias=neg_max[0:64, 0:1], accum_out=row_sum[0:64, 0:1]).then_inc(s_exp, 1)

            def put_mix(j, u):
                act.wait_ge(pv_mm, unit_no(j, u))
                tok, n = P * u, (P if u < SAMPLE_UNIT else DEC)
                for h in range(2):
                    r = slice(64 * h, 64 * h + 64)
                    i = act_copy(mix[r, bass.ds(j, 1), tok:tok + n], pv_ps[r, n * h:n * h + n].rearrange("p (a c) -> p a c", a=1))
                i.then_inc(mix_put, 1)

            def split_cache(j):
                r = 4 * j + W_U + 3
                act.wait_ge(raw_in[1], 16 * (2 * j + 4))
                if not isinstance(j, int) or j > 0:
                    act.wait_ge(pv_mm, UNITS * j)
                raw = w_raw[1][:, :, :].rearrange("p k n -> p (k n)")
                for h in range(2):
                    rr = slice(64 * h, 64 * h + 64)
                    act_copy(kc[h][rr, :], raw[rr, 0:CACHE])
                act_copy(vc_h[:, :, :], raw[:, CACHE:2 * CACHE].rearrange("p (t d) -> p t d", d=P)).then_inc(w_high, 1)

            def slot(j, c, unit, prev):
                if isinstance(j, int) and j == 0 and c == 3:
                    act.wait_ge(u_out[3], 32)
                if c is not None:
                    if c == 0 and not (isinstance(j, int) and j == 0):
                        block_high(j - 1, 8)
                    if isinstance(j, int) and j == 0 and c in (1, 2):
                        put_group(c + 1)
                    if c > 0 and (c - 1) % 3 != Q:
                        block_high(j, c - 1)
                elif unit and unit[1] == 6:
                    block_high(j - 1, 8)
                if prev:
                    turned_high(*prev)
                if c == 8:
                    act.wait_ge(blk_mm, block_no(j, 6))
                    split_high(3 * j + W_U + 3, 0, 0, wh[0])
                if new_pair(j, c, unit):
                    act.wait_ge(blk_mm, block_no(j - 1, 7))
                    split_high(3 * j + W_U + 1, 0, 1, wh[1])
                if c == 1 and not (isinstance(j, int) and j == 0):
                    act.wait_ge(blk_mm, block_no(j - 1, 8))
                    split_high(3 * j + W_U + 2, 0, 0, wh3)
                if c is not None and c % 3 == 2:
                    v_high(j, c - 1)
                if unit:
                    exps(*unit)
                if not unit and c is None:
                    mix_parts(2, 4)
                if prev:
                    put_mix(*prev)
                if c is None and unit and unit[1] == SAMPLE_UNIT:
                    act.wait_ge(pool_put, GROUPS)
                    act.wait_ge(mix_put, UNITS * (PAIRS - 1))
                    act.wait_ge(qs_put, 4 * PAIRS)
                    mix_parts(0, 2)
                if c is not None and c % 3 == 1:
                    block_high(j, c - 1)
                if c == 3:
                    split_cache(j)
                if c is not None and c > 0:
                    store_block(j, c - 1)
                elif c == 0 and not (isinstance(j, int) and j == 0) or c is None and unit and unit[1] == 6:
                    store_block(j - 1, 8)


            act.wait_ge(corners_in, 16 * 2 * N_HEADS)
            attention(act, slot)

            act.wait_ge(mix_put, UNITS * PAIRS)
            mix_parts(4, KT)
            act.wait_ge(k_out, 32 * PAIRS)
            act.wait_ge(v_out, 32 * PAIRS)

            def out_step(d, s):
                ahead(d, s)
                m = d - D_OUT
                act_copy(blocks(y[:, bass.ds(m, 1), :].rearrange("p a t -> p (a t)")), dense_ps(s))
                act.wait_ge(sq_sum, m + 1)
                act.activation(blocks(tmp[:, :]), dense_ps(s), ACT.Square).then_inc(tile_out, 1)

            with act.Fori(0, KT // 2 - 1) as i:
                for s in range(2):
                    out_step(2 * i + (D_OUT + s), s)

            def squares_free(i, b, s):
                if b == 0:
                    act.wait_ge(sq_sum, sum_no(i, KT - 2))
                else:
                    act.wait_ge(sum_blk, pair_no(i, b - 1, s))

            def out_block(b, s):
                wait_pair(act, 0, b, s)
                squares_free(0, b, s)
                act.activation(sq_b[s][:, :], ps[:, NB * s + b, 0:BW], ACT.Square).then_inc(sq_blk, 1)
                i = act_copy(y[:, KT - 2 + s, cols(b)], ps[:, NB * s + b, 0:BW])
                if b == NB - 1:
                    i.then_inc(tile_out, 1)

            def ff_block(b, s):
                if b < NB - 1:
                    act.wait_ge(y_blk, 2 * b + s + 1)
                else:
                    act.wait_ge(tile_out, D_GATE - 1 + s)
                squares_free(1, b, s)
                act.activation(sq_b[s][:, :], y[:, KT - 2 + s, cols(b)], ACT.Square).then_inc(sq_blk, 1)

            def new_x(stage, squares, last_block, d):
                i = stage - 1
                load_root_table()
                last_block(0, 0)
                last_block(0, 1)
                last_block(1, 0)
                root(out_norm, i, 0, ss)
                last_block(1, 1)
                for b in range(NB):
                    for k in range(KT):
                        act.wait_ge(added, x_no(i, b, k))
                        x_parts(stage, b, k, squares)
                        if (b, k) == (0, 2):
                            ahead(d - 2, 0)
                        if (b, k) == (0, 3):
                            last_block(2, 0)
                        if (b, k) == (0, 5):
                            root(out_norm, i, 1, ss)
                        if (b, k) == (0, 7):
                            last_block(2, 1)
                            if stage == 2:
                                act.dma_start(p_raw[:, :, :], p_t).then_inc(p_in, 16)
                                act.dma_start(wp_raw[:, :, :, :], w_ple).then_inc(wp_in, 16)
                            ahead(d - 1, 1)
                        if stage == 2 and (b, k) == (2, 1):
                            act.wait_ge(p_in, 16)
                            act_copy(p_h[:, :, :], p_raw[:, :, :]).then_inc(p_high, 1)
                        if (b, k) == (1, 5):
                            root(out_norm, i, 2, ss)
                        if squares and (b, k) == (1, 3):
                            root(in_norm, 1, 0, rb)
                if squares:
                    root(in_norm, 1, 1, rb)
                    root(in_norm, 1, 2, rb)

            new_x(1, True, out_block, D_FF)

            def hidden_step(d, s, n, m):
                ahead(d, s)
                act.wait_ge(tile_out, d + 1)
                act.activation(tmp[:, :], tmp[:, :], ACT.Square).then_inc(sq_done, 1)
                act.wait_ge(sq_done, n + 1)
                act_copy(mh[:, bass.ds(m, 1), :].rearrange("p a t -> p (a t)"), tmp[:, :]).then_inc(hid_high, 1)

            def ff_chunk(c, last):
                with act.Fori(0, KT // 2) as i:
                    for s in range(2):
                        hidden_step(2 * KT * c + 2 * i + (D_FF + s), s, KT * c + 2 * i + s, 2 * i + s)
                with act.Fori(0, KT // 2 - (1 if last else 0)) as i:
                    for s in range(2):
                        d = 2 * KT * c + 2 * i + (D_FF + KT + s)
                        ahead(d, s)
                        if last:
                            m = 2 * i + s
                            act.wait_ge(tile_out, d + 1)
                            act.wait_ge(sq_sum, m + sum_no(1, 0))
                            act.wait_ge(hid_low, KT * FF_CHUNKS)
                            act.activation(tmp[:, :], y[:, bass.ds(m, 1), :].rearrange("p a t -> p (a t)"), ACT.Square)\
                               .then_inc(sq_put, 1)

            with act.Fori(0, FF_CHUNKS - 1) as c:
                ff_chunk(c, False)
            ff_chunk(FF_CHUNKS - 1, True)

            new_x(2, False, ff_block, D_GATE)
            act.wait_ge(wp_in, 16)

            def split_wp(m, s):
                act_copy(wp_h[s][:, :, :], wp_raw[:, bass.ds(m, 1), :, :].rearrange("p a k n -> p (a k) n"))\
                    .then_inc(wp_high, 1)

            split_wp(0, 0)
            split_wp(1, 1)

            def gate_step(m, s):
                act.wait_ge(tile_mm, m + (D_GATE + 1))
                split_high(m + (D_GATE + 2 + W_OF_D), 0, s, wh[s])
                act.wait_ge(sq_sum, m + sum_no(2, 0))
                act.activation(blocks(tmp[:, :]), dense_ps(s), ACT.Sigmoid).then_inc(gate_put, 1)
                act.wait_ge(gated, NB * m + NB)
                act.activation(tmp[:, :], y[:, bass.ds(m, 1), :].rearrange("p a t -> p (a t)"), ACT.Square)\
                   .then_inc(sq_put, 1)
                split_wp(m + 2, s)

            with act.Fori(0, KT // 2 - 1) as i:
                for s in range(2):
                    gate_step(2 * i + s, s)

            def gate_block(b, s):
                wait_pair(act, 2, b, s)
                if b == 0:
                    act.wait_ge(sq_sum, sum_no(2, KT - 2))
                else:
                    act.wait_ge(gated, NB * (KT - 2) + pair_no(0, b - 1, s))
                act.activation(sig_b[s][:, :], ps[:, NB * s + b, 0:BW], ACT.Sigmoid).then_inc(gate_blk, 1)

            def gated_squares(b, s):
                act.wait_ge(gated, NB * (KT - 2) + pair_no(0, b, s))
                squares_free(2, b, s)
                act.activation(sq_b[s][:, :], y[:, KT - 2 + s, cols(b)], ACT.Square).then_inc(sq_blk, 1)

            for b in range(NB):
                for s in range(2):
                    gate_block(b, s)
                    if b and not s:
                        root(out_norm, 2, b - 1, ss)
                    gated_squares(b, s)
            load_root_table()
            root(out_norm, 2, NB - 1, ss)

        @block.vector
        def _(dve):
            def sub(out, a, b):
                return dve.tensor_tensor(out, a, b, ALU.subtract)

            def split_low(r, s, hi, lo):
                dve.wait_ge(w_high, r + 1)
                sub(lo[:, :, :], w_raw[s][:, :, :], hi[:, :, :]).then_inc(w_low, 1)

            def ahead(d, s):
                dve.wait_ge(tile_mm, d + 1)
                split_low(d + 2 + R_OF_D, s, wh[s], wl[s])

            def inverse(norm, i, b, t):
                dve.wait_ge(norm[1], norm_no(i, b))
                dve.reciprocal(t[:, cols(b)], t[:, cols(b)]).then_inc(norm[2], 1)
                dve.wait_ge(norm[2], norm_no(i, b))

            for i in range(HIST):
                last = dve.memset(inv_n[:, i:i + 1], 1.0 / (i + 1))
            last.then_inc(u_run, 1)
            for b in range(NB):
                for k in range(KT):
                    dve.wait_ge(x_high, x_no(0, b, k))
                    sub(xl[:, k, cols(b)], y[:, k, cols(b)], xh[:, k, cols(b)]).then_inc(x_low, 1)
                    if k % 2:
                        dve.tensor_tensor(xsq[:, k, cols(b)], y[:, k, cols(b)], y[:, k, cols(b)], ALU.mult)\
                           .then_inc(x_odd, 1)
                    if b == 0 and k in (0, 4):
                        split_low(k // 4, k // 4, wh[k // 4], wl[k // 4])
            for b in range(NB - 1):
                inverse(in_norm, 0, b, rb)
            dve.wait_ge(x_low, NB * KT)
            dve.wait_ge(x_even, NB * KT // 2)
            dve.wait_ge(x_odd, NB * KT // 2)
            for u_ext in u_exts:
                last = dve.memset(u_ext[:, 0:HIST], 0.0)
            last.then_inc(u_run, 1)
            inverse(in_norm, 0, NB - 1, rb)
            dve.wait_ge(state_in, 16)

            S0 = HIST + SEQ

            def put_u(g):
                dve.wait_ge(tile_mm, g + 1)
                src = ps[:, NB * (g % 2):NB * (g % 2) + NB, :]
                u_ext = u_exts[g % 3]
                if g == 3:
                    dve.wait_ge(u_out[0], 32)
                    dve.wait_ge(u_diff, 1)
                dve.tensor_tensor(u_ext[:, HIST:HIST + 2 * BW].rearrange("p (a b) -> p a b", a=2), src[:, 0:2, 0:BW],
                                  rb[:, 0:2 * BW].rearrange("p (a b) -> p a b", a=2), ALU.mult)
                dve.tensor_tensor(u_ext[:, HIST + 2 * BW:S0], src[:, 2, 0:BW - DEC], rb[:, 2 * BW:SEQ], ALU.mult)
                dve.tensor_tensor(u_ext[:, S0 + HIST:UCOLS], src[:, 2, BW - DEC:BW], rb[:, SEQ:TOK], ALU.mult)
                dve.tensor_copy(u_ext[:, S0:S0 + HIST], state[:, g, :]).then_inc(tile_out, 1)
                split_low(g + 2, g % 2, wh[g % 2], wl[g % 2])
                if g == GROUPS - 1:
                    split_low(W_U + 2, 0, wh3, wl3)

            def pool_group(g):
                w = POOL_WINDOWS[g]
                u_ext = u_exts[g % 3]
                runs = 2 + 2 * g + g * (g + 1) // 2
                dve.wait_ge(tile_out, g + 1)
                dve.wait_ge(u_run, runs)
                a, shift, i = u_ext, 1, 0
                while shift < w:
                    o = run_sum[i % 2]
                    dve.tensor_tensor(o[:, shift:UCOLS], a[:, shift:UCOLS], a[:, 0:UCOLS - shift], ALU.add)
                    dve.tensor_copy(o[:, 0:shift], a[:, 0:shift]).then_inc(u_run, 1)
                    runs += 1
                    dve.wait_ge(u_run, runs)
                    a, shift, i = o, 2 * shift, i + 1
                if g:
                    dve.wait_ge(pool_mm, g)
                for o0, c0, n in ((0, HIST, SEQ), (SEQ, S0 + HIST, DEC)):
                    last = dve.scalar_tensor_tensor(out=diff[:, o0:o0 + n], in0=a[:, c0:c0 + n], scalar=1.0 / w,
                                                    in1=u_ext[:, c0:c0 + n], op0=ALU.mult, op1=ALU.subtract)
                last.then_inc(u_run, 1)
                runs += 1
                dve.wait_ge(u_run, runs)
                dve.tensor_tensor(diff[:, 0:w - 1], a[:, HIST:HIST + w - 1], inv_n[:, 0:w - 1], ALU.mult)\
                    .then_inc(u_run, 1)
                runs += 1
                dve.wait_ge(u_run, runs)
                sub(diff[:, 0:w - 1], diff[:, 0:w - 1], u_ext[:, HIST:HIST + w - 1]).then_inc(u_diff, 1)

            put_u(0)
            put_u(1)
            pool_group(0)
            pool_group(1)
            put_u(2)
            pool_group(2)
            put_u(3)
            pool_group(3)

            def block_t(j, c):
                t, b = c % 3, c // 3
                tok, n = ABLK[b]
                dve.wait_ge(blk_mm, block_no(j, c))
                stores = k_out if t == K else v_out
                if t == Q and not (isinstance(j, int) and j == 0 and b == 0):
                    dve.wait_ge(q_dup, 6 * j + 2 * b)
                if t != Q:
                    if b == 2:
                        dve.wait_ge(stores, 32 * j + 16)
                    elif b == 0 and not (isinstance(j, int) and j == 0):
                        dve.wait_ge(stores, 32 * j)
                    dve.tensor_tensor(tb[:, t, 0:n], ps[:, c % 2, 0:n], rb[:, tok:tok + n], ALU.mult).then_inc(blk_t, 1)
                else:
                    dve.scalar_tensor_tensor(out=tb[:, t, 0:n], in0=ps[:, c % 2, 0:n], scalar=QSCALE,
                                             in1=rb[:, tok:tok + n], op0=ALU.mult, op1=ALU.mult).then_inc(blk_t, 1)

            def block_low(j, c):
                t, b = c % 3, c // 3
                tok, n = ABLK[b]
                dve.wait_ge(blk_t, block_no(j, c))
                if t == K:
                    for h in range(2):
                        r, o = slice(64 * h, 64 * h + 64), slice(64 - 64 * h, 128 - 64 * h)
                        dve.wait_ge(blk_high, high_no(j, c, h))
                        i = sub(kk[h][o, tok:tok + n], tb[r, K, 0:n], kk[h][r, tok:tok + n])
                    i.then_inc(blk_low, 1)
                else:
                    for h in range(2):
                        r = slice(64 * h, 64 * h + 64)
                        dve.wait_ge(blk_high, high_no(j, c, h))
                        i = sub(q_l[h][r, b % 2, 0:n], tb[r, Q, 0:n], q_h[h][r, b % 2, 0:n])
                    i.then_inc(blk_low, 1)

            def v_low(j, c):
                b = c // 3
                dve.wait_ge(blk_high, high_no(j, c, 0))
                if b < 2:
                    sub(v_l[:, 3 * b:3 * b + 3, :], ps[:, c % 2, 0:384].rearrange("p (t d) -> p t d", d=P),
                        v_h[:, 3 * b:3 * b + 3, :]).then_inc(blk_low, 1)
                else:
                    sub(v_l[:, 6:8, :], ps[:, c % 2, 0:256].rearrange("p (t d) -> p t d", d=P), v_h[:, 6:8, :])
                    sub(v_l[0:DEC, 8, :], ps[0:DEC, c % 2, 256:384], v_h[0:DEC, 8, :]).then_inc(blk_low, 1)

            def turned_low(j, u):
                cols = 256 if u < SAMPLE_UNIT else 64
                p = parts(n_tiles(u))
                for n, (i0, i1) in enumerate(p):
                    dve.wait_ge(t_high, turned_no(j, u) - (len(p) - 1 - n))
                    sub(pt_l[:, i0:i1, 0:cols], turned[:, i0:i1, 0:cols], pt_h[:, i0:i1, 0:cols]).then_inc(t_low, 1)

            def maxima(j, u):
                dve.wait_ge(s_mm, head_no(j, u, 0))
                if u == 0:
                    dve.wait_ge(bias_in, 16 * j + 16)
                if u == SAMPLE_UNIT:
                    dve.wait_ge(bias_s_in, 32 * j + 32)
                if not (isinstance(j, int) and j == 0 and u == 0):
                    dve.wait_ge(t_mm, turned_no(j, u - 1) if u > 0 else turned_no(j - 1, 8))
                apart(dve)
                if u < SAMPLE_UNIT:
                    lo = WIN - P * n_tiles(u)
                    for h in range(2):
                        if h == 1:
                            dve.wait_ge(s_mm, head_no(j, u, 1))
                            apart(dve)
                        c0 = score_cols(h)
                        dve.tensor_tensor_reduce(out=prob[:, h, lo:WIN], in0=flat[:, c0 + lo:c0 + WIN],
                                                 in1=bias[:, h, lo:WIN], scale=-1.0, scalar=3.0e38, op0=ALU.add,
                                                 op1=ALU.min, accum_out=neg_max[:, h:h + 1]).then_inc(s_max, 1)
                else:
                    dve.tensor_tensor_reduce(out=prob[0:64, 0, 0:SKEYS],
                                             in0=flat[0:64, SAMPLE_COL:SAMPLE_COL + SKEYS],
                                             in1=bias_s[0:64, :], scale=-1.0, scalar=3.0e38, op0=ALU.add,
                                             op1=ALU.min, accum_out=neg_max[0:64, 0:1]).then_inc(s_max, 1)

            def inverses(j, u):
                rows = P if u < SAMPLE_UNIT else 64
                dve.wait_ge(s_exp, head_no(j, u, 0))
                dve.reciprocal(inv_sum[0:rows, 0:1], row_sum[0:rows, 0:1]).then_inc(s_inv[0], 1)
                if u < SAMPLE_UNIT:
                    dve.wait_ge(s_exp, head_no(j, u, 1))
                    dve.reciprocal(inv_sum[:, 1:2], row_sum[:, 1:2]).then_inc(s_inv[1], 1)
                    dve.wait_ge(s_inv[1], second_no(j, u))
                    apart(dve)
                    pr = prob[:, 1, WIN - P * n_tiles(u):WIN]
                    dve.tensor_scalar(pr, pr, inv_sum[:, 1:2], 1.0, ALU.mult, ALU.mult).then_inc(s_norm[1], 1)

            def split_cache(j):
                dve.wait_ge(w_high, 4 * j + W_U + 4)
                raw = w_raw[1][:, :, :].rearrange("p k n -> p (k n)")
                for h in range(2):
                    r, o = slice(64 * h, 64 * h + 64), slice(64 - 64 * h, 128 - 64 * h)
                    sub(kc[h][o, :], raw[r, 0:CACHE], kc[h][r, :])
                sub(vc_l[:, :, :], raw[:, CACHE:2 * CACHE].rearrange("p (t d) -> p t d", d=P), vc_h[:, :, :])\
                    .then_inc(w_low, 1)

            def mix_parts(n0, n1):
                for n in range(n0, n1):
                    k = MIX_ORDER[n]
                    dve.wait_ge(mix_high, n + 1)
                    sub(ml[:, k, :], mix[:, k, :], mh[:, k, :]).then_inc(mix_low, 1)

            def slot(j, c, unit, prev):
                if c is not None:
                    if c == 0 and not (isinstance(j, int) and j == 0):
                        block_t(j - 1, 8)
                        block_low(j - 1, 8)
                    if c > 0:
                        block_t(j, c - 1)

                        if (c - 1) % 3 == K:
                            block_low(j, c - 1)
                elif unit and unit[1] == 6:
                    block_t(j - 1, 8)
                    block_low(j - 1, 8)
                if prev:
                    turned_low(*prev)
                if c == 8:
                    split_low(4 * j + W_U + 4, 0, wh[0], wl[0])
                if new_pair(j, c, unit):
                    split_low(4 * j + W_U + 1, 1, wh[1], wl[1])
                if c == 1 and not (isinstance(j, int) and j == 0):
                    split_low(4 * j + W_U + 2, 0, wh3, wl3)
                if c is not None and c % 3 == 2:
                    v_low(j, c - 1)
                if unit:
                    maxima(*unit)
                    inverses(*unit)
                if c is None and prev[1] >= SAMPLE_UNIT - 1:
                    mix_parts(2 * (prev[1] - SAMPLE_UNIT + 1), 2 * (prev[1] - SAMPLE_UNIT + 2))
                if c is not None and (c - 1) % 3 == Q:
                    block_low(j, c - 1)
                if c == 3:
                    split_cache(j)

            attention(dve, slot)

            mix_parts(4, KT)

            with dve.Fori(0, KT // 2 - 1) as i:
                for s in range(2):
                    ahead(2 * i + (D_OUT + s), s)

            def scale(g, b, k):
                return dve.scalar_tensor_tensor(out=y[:, k, cols(b)], in0=y[:, k, cols(b)], scalar=vec[:, g, k:k + 1],
                                                in1=ss[:, cols(b)], op0=ALU.mult, op1=ALU.mult).then_inc(scaled, 1)

            def new_x(stage, g, last_block, d, in_i=None):
                i = stage - 1
                if last_block:
                    last_block(0, 0)
                    last_block(0, 1)
                    last_block(1, 0)
                inverse(out_norm, i, 0, ss)
                if last_block:
                    last_block(1, 1)
                for n in range(NB * KT + 2):
                    b, k = n // KT, n % KT
                    if b < NB:
                        scale(g, b, k)
                    if (b, k) == (0, 4):
                        ahead(d - 2, 0)
                        if last_block:
                            last_block(2, 0)
                    if (b, k) == (0, 7) and last_block:
                        last_block(2, 1)
                    if n >= 2:
                        lb, lk = (n - 2) // KT, (n - 2) % KT
                        dve.wait_ge(x_high, x_no(stage, lb, lk))
                        sub(xl[:, lk, cols(lb)], y[:, lk, cols(lb)], xh[:, lk, cols(lb)]).then_inc(x_low, 1)
                    if k == KT - 1 and b < NB - 1:
                        inverse(out_norm, i, b + 1, ss)
                    if (b, k) == (1, 0):
                        ahead(d - 1, 1)
                if in_i:
                    for b in range(NB):
                        inverse(in_norm, in_i, b, rb)

            new_x(1, 0, None, D_FF, 1)

            def hidden_step(d, s, n, m):
                dve.wait_ge(tile_mm, d + 1)
                if not (isinstance(n, int) and n == 0):
                    dve.wait_ge(hid_low, n)
                    dve.wait_ge(hid_high, n)
                dve.scalar_tensor_tensor(out=blocks(tmp[:, :]), in0=dense_ps(s), scalar=0.0, in1=blocks(rb[:, :]),
                                         op0=ALU.max, op1=ALU.mult).then_inc(tile_out, 1)
                ahead(d, s)
                dve.wait_ge(hid_high, n + 1)
                sub(ml[:, bass.ds(m, 1), :].rearrange("p a t -> p (a t)"), tmp[:, :],
                    mh[:, bass.ds(m, 1), :].rearrange("p a t -> p (a t)")).then_inc(hid_low, 1)

            def ff_chunk(c, peel=False, last=False):
                if peel:
                    hidden_step(2 * KT * c + D_FF, 0, KT * c, 0)
                    hidden_step(2 * KT * c + D_FF + 1, 1, KT * c + 1, 1)
                with dve.Fori(1 if peel else 0, KT // 2) as i:
                    for s in range(2):
                        hidden_step(2 * KT * c + 2 * i + (D_FF + s), s, KT * c + 2 * i + s, 2 * i + s)
                with dve.Fori(0, KT // 2 - (1 if last else 0)) as i:
                    for s in range(2):
                        d = 2 * KT * c + 2 * i + (D_FF + KT + s)
                        ahead(d, s)
                        ym = blocks(y[:, bass.ds(2 * i + s, 1), :].rearrange("p a t -> p (a t)"))
                        if peel:
                            dve.tensor_copy(ym, dense_ps(s)).then_inc(tile_out, 1)
                        else:
                            dve.wait_ge(tile_out, d - KT)
                            dve.tensor_tensor(ym, ym, dense_ps(s), ALU.add).then_inc(tile_out, 1)

            ff_chunk(0, True)
            with dve.Fori(1, FF_CHUNKS - 1) as c:
                ff_chunk(c)
            ff_chunk(FF_CHUNKS - 1, last=True)

            def ff_block(b, s):
                wait_pair(dve, 1, b, s)
                if b == 0:
                    dve.wait_ge(tile_out, D_GATE - 2 * KT - 1 + s)
                ym = y[:, KT - 2 + s, cols(b)]
                dve.tensor_tensor(ym, ym, ps[:, NB * s + b, 0:BW], ALU.add)\
                   .then_inc(y_blk if b < NB - 1 else tile_out, 1)

            def wp_part(m, s):
                dve.wait_ge(wp_high, m + 1)
                sub(wp_l[s][:, :, :], wp_raw[:, bass.ds(m, 1), :, :].rearrange("p a k n -> p (a k) n"),
                    wp_h[s][:, :, :]).then_inc(wp_low, 1)

            new_x(2, 1, ff_block, D_GATE)
            dve.wait_ge(p_high, 1)
            sub(p_l[:, :, :], p_raw[:, :, :], p_h[:, :, :]).then_inc(p_low, 1)
            wp_part(0, 0)
            wp_part(1, 1)

            def gate_step(m, s):
                ahead(m + D_GATE, s)
                dve.wait_ge(gate_put, m + 1)
                for b in range(NB):
                    dve.wait_ge(ple_mm, NB * m + b + 1)
                    dve.tensor_tensor(y[:, bass.ds(m, 1), cols(b)].rearrange("p a t -> p (a t)"),
                                      ps[:, 6 + (s + b) % 2, 0:BW], tmp[:, cols(b)], ALU.mult).then_inc(gated, 1)
                wp_part(m + 2, s)

            with dve.Fori(0, KT // 2 - 1) as i:
                for s in range(2):
                    gate_step(2 * i + s, s)

            def gate_block(b, s):
                dve.wait_ge(gate_blk, pair_no(0, b, s))
                dve.wait_ge(ple_mm, NB * (KT - 2) + pair_no(0, b, s))
                dve.tensor_tensor(y[:, KT - 2 + s, cols(b)], ps[:, 6 + s, 0:BW], sig_b[s][:, :], ALU.mult)\
                   .then_inc(gated, 1)

            def last_norm(b):
                inverse(out_norm, 2, b, ss)

            def last_x(b, k0, k1):
                for k in range(k0, k1):
                    scale(2, b, k)
                    if k in DVE_ADDS:
                        dve.wait_ge(scaled, x_no(2, b, k))
                        yk = y[:, k, cols(b)]
                        dve.tensor_tensor(yk, yk, xsum2[:, k, cols(b)], ALU.add).then_inc(added2, 1)

            gate_block(0, 0)
            gate_block(0, 1)
            gate_block(1, 0)
            last_norm(0)
            gate_block(1, 1)
            dve.wait_ge(xsum_put, 3 * KT)
            last_x(0, 0, 5)
            gate_block(2, 0)
            last_x(0, 5, KT)
            last_norm(1)
            last_x(1, 0, 2)
            gate_block(2, 1)
            last_x(1, 2, 6)
            last_norm(2)
            last_x(1, 6, KT)
            last_x(2, 0, KT)

        @block.gpsimd
        def _(pool):
            pool.memset(ones[:, :], 1.0).then_inc(const_made, 1)
            pool.memset(ident[:, :], 0.0).then_inc(const_made, 1)
            pool.memset(neg[:, :], NEG).then_inc(const_made, 1)
            pool.wait_ge(const_made, 2)
            pool.affine_select(out=ident[:, :], in_=ident[:, :], compare_op=ALU.not_equal, fill=1.0, base=0,
                               pattern=[[-1, P]], channel_multiplier=1).then_inc(const_made, 1)
            pool.memset(q_s[:, :, :, :].bitcast(F32), 0.0).then_inc(qs_zero, 1)
            pool.memset(eps[:, :], EPS).then_inc(const_made, 1)
            pool.wait_ge(gains_in, 16)

            def gain_tile(arrived, s, row):
                pool.wait_ge(raw_in[s], 16 * arrived)
                apart(pool)
                g = gain[:, bass.ds(row, 1), :].rearrange("p a k -> p (a k)").unsqueeze(2).to_broadcast([P, KT, P])
                pool.tensor_tensor(w_raw[s][:, :, :], w_raw[s][:, :, :], g, ALU.mult).then_inc(w_gained, 1)

            gain_tile(1, 0, 0)
            gain_tile(1, 1, 0)
            for b in range(NB):
                for k in range(1, KT):
                    pool.wait_ge(x_even, (KT * b + k) // 2 + 1)
                    pool.wait_ge(x_odd, (KT * b + k + 1) // 2)
                    n = (KT - 1) * b + k - 1
                    if n:
                        pool.wait_ge(x_sums, n)
                    pool.tensor_tensor(xsq[:, 0, cols(b)], xsq[:, 0, cols(b)], xsq[:, k, cols(b)], ALU.add)\
                        .then_inc(x_sums, 1)
                if b == 1:
                    gain_tile(2, 0, 0)
            for w in range(3, W_U + 3):
                gain_tile(w // 2 + 1, w % 2, 0)

            def scale_rows(j, u):
                whole = u < SAMPLE_UNIT
                pool.wait_ge(s_inv[0], unit_no(j, u))
                apart(pool)
                lo = WIN - P * n_tiles(u)
                pr = prob[:, 0, lo:WIN] if whole else prob[0:64, 0, 0:SKEYS]
                iv = inv_sum[:, 0:1] if whole else inv_sum[0:64, 0:1]
                pool.tensor_scalar(pr, pr, iv, 1.0, ALU.mult, ALU.mult).then_inc(s_norm[0], 1)

            def queries_low(j, c, unit):
                b, n = c // 3, ABLK[c // 3][1]
                if unit:
                    pool.wait_ge(s_norm[0], unit_no(*unit))
                pool.wait_ge(blk_high, high_no(j, c, 3))
                apart(pool)
                for h in range(2):
                    r, o = slice(64 * h, 64 * h + 64), slice(64 - 64 * h, 128 - 64 * h)
                    pool.tensor_tensor(q_l[h][o, b % 2, 0:n], tb[r, Q, 0:n], q_h[h][r, b % 2, 0:n], ALU.subtract)\
                        .then_inc(q_dup, 1)
                    pool.wait_ge(q_dup, 6 * j + 2 * b + h + 1)
                apart(pool)

            def place_queries(j):
                pool.wait_ge(blk_low, block_no(j, 6 + Q))
                pool.wait_ge(blk_high, high_no(j, 6 + Q, 3))
                pool.wait_ge(q_dup, 6 * j + 6)
                if isinstance(j, int) and j == 0:
                    pool.wait_ge(qs_zero, 1)
                else:
                    pool.wait_ge(s_mm, head_no(j - 1, 8, 0))
                apart(pool)
                for part, q in enumerate((q_h, q_l)):
                    for h in range(2):
                        pool.tensor_copy(q_s[:, part, h, DEC * h:DEC * h + DEC], q[h][:, 0, 256:256 + DEC])\
                            .then_inc(qs_put, 1)

            def slot(j, c, unit, prev):
                if unit:
                    if unit[1] == 6:
                        place_queries(unit[0])
                    scale_rows(*unit)
                if c is not None and c % 3 == 1:
                    queries_low(j, c - 1, unit)
                if c in (5, 6):
                    gain_tile(2 * j + 5, c - 5, j + 1)
                if new_pair(j, c, unit):
                    gain_tile(2 * j + 4, 0, j)

            attention(pool, slot)

            def sum_squares(n):
                pool.wait_ge(sq_sum, n)
                pool.tensor_tensor(ss[:, :], ss[:, :], tmp[:, :], ALU.add).then_inc(sq_sum, 1)

            def sum_block(i, b, s):
                pool.wait_ge(sq_blk, pair_no(i, b, s))
                pool.wait_ge(sq_sum, sum_no(i, KT - 2))
                if s:
                    pool.wait_ge(sum_blk, pair_no(i, b, 0))
                pool.tensor_tensor(ss[:, cols(b)], ss[:, cols(b)], sq_b[s][:, :], ALU.add).then_inc(sum_blk, 1)

            def sum_parts(out, m, n):
                o = out[:, bass.ds(m, 1), :].rearrange("p a t -> p (a t)")
                pool.tensor_tensor(o, xh[:, bass.ds(m, 1), :].rearrange("p a t -> p (a t)"),
                                   xl[:, bass.ds(m, 1), :].rearrange("p a t -> p (a t)"), ALU.add).then_inc(xsum_put, 1)

            pool.wait_ge(blk_mm, BLOCKS * PAIRS)
            pool.memset(ss[:, :], 0.0).then_inc(sq_sum, 1)

            def dense_gain(i, s):
                gain_tile(i + (D_OUT + R_OF_D) // 2 + 2 + s, 1 - s, i + PAIRS + 1 + s)

            with pool.Fori(0, KT // 2 - 1) as i:
                for s in range(2):
                    dense_gain(i, s)
                    m = 2 * i + s
                    sum_parts(xsum, m, m)
                    pool.wait_ge(tile_out, m + D_OUT + 1)
                    sum_squares(m + 1)

            def add_x(i, b, k, parts):
                pool.wait_ge(scaled, x_no(i, b, k))
                yk = y[:, k, cols(b)]
                pool.tensor_tensor(yk, yk, parts[:, k, cols(b)], ALU.add).then_inc(added, 1)

            def new_x(stage, parts, d):
                i = stage - 1
                dense_gain((d - D_OUT) // 2 - 1, 0)
                sum_block(i, 0, 0)
                sum_block(i, 0, 1)
                sum_parts(parts, KT - 2, KT - 2)
                sum_block(i, 1, 0)
                sum_parts(parts, KT - 1, KT - 1)
                pool.wait_ge(xsum_put, KT * stage)
                for b in range(NB):
                    for k in range(KT):
                        add_x(i, b, k, parts)
                        if (b, k) == (0, 0):
                            sum_block(i, 1, 1)
                        if (b, k) == (0, 4):
                            sum_block(i, 2, 0)
                        if (b, k) == (0, 7):
                            sum_block(i, 2, 1)
                    if b == 1:
                        dense_gain((d - D_OUT) // 2 - 1, 1)

            new_x(1, xsum, D_FF)
            pool.memset(ss[:, :], 0.0).then_inc(sq_sum, 1)
            with pool.Fori(KT // 2, (D_GATE - D_OUT - KT) // 2) as i:
                for s in range(2):
                    dense_gain(i, s)
            pool.wait_ge(tile_mm, D_GATE - KT)
            with pool.Fori((D_GATE - D_OUT - KT) // 2, (D_GATE - D_OUT) // 2 - 1) as i:
                for s in range(2):
                    dense_gain(i, s)
                    m = 2 * i + (s - (D_GATE - D_OUT - KT))
                    sum_parts(xsum, m, m)
                    pool.wait_ge(sq_put, m + 1)
                    sum_squares(m + sum_no(1, 0))
            new_x(2, xsum, D_GATE)
            pool.memset(ss[:, :], 0.0).then_inc(sq_sum, 1)
            pool.wait_ge(p_low, 1)
            pool.wait_ge(x_low, 3 * NB * KT)
            for m in range(KT - 2):
                if m < KT - 3:
                    dense_gain((D_GATE - D_OUT + m) // 2, m % 2)
                sum_parts(xsum2, m, m)
                pool.wait_ge(sq_put, KT - 2 + m + 1)
                sum_squares(sum_no(2, m))
            for m in (KT - 2, KT - 1):
                sum_parts(xsum2, m, m)

            for b, s in ((0, 0), (0, 1), (1, 0), (1, 1)):
                sum_block(2, b, s)
            pool.wait_ge(xsum_put, 3 * KT)
            for b in range(NB):
                for k in range(KT):
                    if (b, k) == (0, 5):
                        sum_block(2, 2, 0)
                    if (b, k) == (1, 2):
                        sum_block(2, 2, 1)
                    if k not in DVE_ADDS:
                        pool.wait_ge(scaled, x_no(2, b, k))
                        yk = y[:, k, cols(b)]
                        pool.tensor_tensor(yk, yk, xsum2[:, k, cols(b)], ALU.add).then_inc(added, 1)


def kernel(**inputs):
    import numpy as np
    import concourse.bacc as bacc
    from concourse.bass_utils import run_bass_kernel_spmd

    a = {k: np.asarray(v) for k, v in inputs.items()}
    one = np.float32(1)

    def feature_major(prompt, sample):
        return np.concatenate([prompt, sample], 0).T.reshape(-1, P, TOK)

    def tiles(w):
        k, m = w.shape
        return w.reshape(k // P, P, m // P, P).transpose(2, 1, 0, 3).reshape(m // P, P, -1)

    w_in = tiles(a["w_in"][0])
    q, k, v, u = (w_in[4 * i:4 * i + 4] for i in range(4))
    cache_k = a["cache_k"][0, 0].transpose(1, 2, 0).reshape(PAIRS, P, CACHE)
    cache_v = a["cache_v"][0, 0].reshape(4, P, PAIRS, P).transpose(2, 1, 0, 3).reshape(PAIRS, P, CACHE)
    cache = np.concatenate([cache_k, cache_v], 2)
    stream = [u] + [t[j:j + 1] for j in range(PAIRS) for t in (q, v, k, cache)] + [tiles(a["w_out"][0])]
    ff1, ff2 = tiles(a["w_ff1"][0]), a["w_ff2"][0]
    for c in range(FF_CHUNKS):
        stream += [ff1[KT * c:KT * c + KT], tiles(ff2[D_MODEL * c:D_MODEL * c + D_MODEL])]
    stream.append(tiles(a["w_ple_gate"][0]))
    w_stream = np.concatenate(stream, 0)

    def columns(g):
        return g.reshape(-1, P).T

    none = np.full((P, KT), one)
    rows = [columns(a["g_mix_pre"][0])] * PAIRS + [none] * 4
    rows += ([columns(a["g_ff_pre"][0])] * 4 + [none] * 4) * FF_CHUNKS + [none] * 4
    gains = np.stack(rows, 1)
    scale = np.concatenate([columns(a["pool_scale"][0]), np.zeros((P, KT - GROUPS), np.float32)], 1)
    vecs = np.stack([columns(a[g][0]) for g in ("g_mix_post", "g_ff_post", "g_ple_post")] + [scale], 1)
    rel = a["rel_bias"][0]
    bias_ext = np.concatenate([np.repeat(rel[:, 256:257], LEFT - 1, 1), rel[:, 256:0:-1]], 1)
    arrays = {
        "x_t": feature_major(a["x_prompt"][0], a["x_sample"][0]),
        "p_t": feature_major(a["p_prompt"][0, 0], a["p_sample"][0, 0]).transpose(1, 0, 2),
        "w_stream": w_stream,
        "w_ple": tiles(a["w_ple"][0]).reshape(KT, P, 2, P).transpose(1, 0, 2, 3),
        "gains": gains,
        "vecs": vecs,
        "w_pool": a["w_pool"][0].transpose(1, 0, 2),
        "state_t": a["state_pool"][0, 0].T.reshape(GROUPS, P, HIST).transpose(1, 0, 2),
        "bias_ext": bias_ext,
    }
    arrays = {n: np.ascontiguousarray(x) for n, x in arrays.items()}
    outs = {"y_t": (KT, P, TOK), "k_new": (PAIRS, P, CACHE + DEC), "v_new": (PAIRS, P, CACHE + DEC),
            "pool_p": (GROUPS, P, HIST), "pool_s": (GROUPS, P, HIST)}
    nc = bacc.Bacc("TRN2", target_bir_lowering=False, num_devices=1)
    args = {n: nc.dram_tensor(n, x.shape, mybir.dt.from_np(x.dtype), kind="ExternalInput").ap()
            for n, x in arrays.items()}
    args |= {n: nc.dram_tensor(n, s, F32, kind="ExternalOutput").ap() for n, s in outs.items()}
    build(nc, **args)
    got = run_bass_kernel_spmd(nc, [arrays], core_ids=[0]).results[0]
    y = got["y_t"].reshape(D_MODEL, TOK).T
    k, v = (got[n].reshape(N_HEADS, HEAD, CACHE + DEC).transpose(2, 0, 1) for n in ("k_new", "v_new"))
    pp, pq = (got[n].reshape(GROUPS * P, HIST).T for n in ("pool_p", "pool_s"))
    return (y[None, :SEQ], y[None, SEQ:], k[None, None, :CACHE], v[None, None, :CACHE], pp[None, None],
            k[None, None, CACHE:], v[None, None, CACHE:], pq[None, None])
```
